# Optimizing a Trainium2 kernel written in Bass

```python
import math
import jax
import jax.numpy as jnp
from jax import lax
import numpy as np

D_MODEL = 1024
BATCH = 1
SEQ = 512
DEPTH = 2
DEC_BATCH = 1
DEC_SEQ = 32
PAST_LEN = 256

CHUNK = 64
Q_BLOCK = 128
EPS = 1e-6
ROPE_BASE = 10000.0
F32 = jnp.float32
N_AB = DEPTH // 2
N_CD = DEPTH // 2
RET_HEADS = 4
RET_DK = 64
RET_DV = 128
SB_HEADS = 8
SB_DH = 64
BAND_HEADS = 8
BAND_DH = 64
BAND_CHUNKS = 8
BAND_WINDOW = BAND_CHUNKS * CHUNK
REL_CLIP = 128
SSD_HEADS = 8
SSD_P = 64
SSD_GROUPS = 2
SSD_N = 128
SSD_CONV = 4
SSD_INNER = SSD_HEADS * SSD_P
SSD_CONV_DIM = SSD_INNER + 2 * SSD_GROUPS * SSD_N
D_FF = 2816
RET_QK_W = RET_HEADS * RET_DK
RET_V_W = RET_HEADS * RET_DV
SB_W = SB_HEADS * SB_DH
BAND_W = BAND_HEADS * BAND_DH
AB_IN = 2 * RET_QK_W + 2 * RET_V_W + 3 * SB_W
AB_OUT = RET_V_W + SB_W
CD_IN = 3 * BAND_W + SSD_INNER + SSD_CONV_DIM + SSD_HEADS
CD_OUT = BAND_W + SSD_INNER

kernel_name = 'hybrid_streaming_encoder_step'

def rms_norm(x, g):
    xf = x.astype(F32)
    y = xf * lax.rsqrt(jnp.mean(xf * xf, axis=-1, keepdims=True) + EPS)
    return (y * g.astype(F32)).astype(x.dtype)

def swiglu(x, w_in, w_out):
    gate, up = jnp.split(x @ w_in, 2, axis=-1)
    return (jax.nn.silu(gate) * up) @ w_out

def rotary(x, pos):
    half = x.shape[-1] // 2
    inv = jnp.power(ROPE_BASE, -jnp.arange(half, dtype=F32) / half)
    ang = pos.astype(F32)[:, None] * inv[None, :]
    cos = jnp.cos(ang)[None, :, None, :]
    sin = jnp.sin(ang)[None, :, None, :]
    xf = x.astype(F32)
    x1, x2 = xf[..., :half], xf[..., half:]
    return jnp.concatenate([x1 * cos - x2 * sin, x1 * sin + x2 * cos], axis=-1).astype(x.dtype)

def retention(q, k, v, state0):
    bsz, L, H, _ = q.shape
    c = min(CHUNK, L)
    n = L // c
    lg = jnp.log1p(-jnp.exp2(-5.0 - jnp.arange(H, dtype=F32)))
    idx = jnp.arange(c, dtype=F32)
    diff = idx[:, None] - idx[None, :]
    dmask = jnp.where(diff >= 0, jnp.exp(lg[:, None, None] * jnp.maximum(diff, 0.0)), 0.0)
    q_dec = jnp.exp(lg[None, :] * (idx[:, None] + 1.0))
    k_dec = jnp.exp(lg[None, :] * (c - 1.0 - idx[:, None]))
    c_dec = jnp.exp(lg * c)

    def chunks(t):
        return jnp.moveaxis(t.astype(F32).reshape(bsz, n, c, H, t.shape[-1]), 1, 0)

    def step(S, inp):
        qi, ki, vi = inp
        att = jnp.einsum('bihd,bjhd->bhij', qi, ki) * dmask
        o = jnp.einsum('bhij,bjhe->bihe', att, vi) + jnp.einsum('bihd,bhde->bihe', qi, S) * q_dec[None, :, :, None]
        S = S * c_dec[None, :, None, None] + jnp.einsum('bjhd,bjhe->bhde', ki * k_dec[None, :, :, None], vi)
        return S, o

    S, o = lax.scan(step, state0.astype(F32), (chunks(q), chunks(k), chunks(v)))
    return jnp.moveaxis(o, 0, 1).reshape(bsz, L, H, -1), S

def stick_breaking(q, k, v, q_pos, k_pos):
    z = jnp.einsum('bqhd,bkhd->bhqk', q, k).astype(F32) * (q.shape[-1] ** -0.5)
    mask = k_pos[None, :] < q_pos[:, None]
    log_1mb = jnp.where(mask, jax.nn.log_sigmoid(-z), 0.0)
    later = lax.cumsum(log_1mb, axis=3, reverse=True) - log_1mb
    w = jnp.where(mask, jnp.exp(jax.nn.log_sigmoid(z) + later), 0.0)
    return jnp.einsum('bhqk,bkhd->bqhd', w, v.astype(F32))

def stick_breaking_blocks(q, k, v):
    bsz, L, H, d = q.shape
    pos = jnp.arange(L, dtype=jnp.int32)

    def blk(i):
        s0 = i * Q_BLOCK
        qb = lax.dynamic_slice_in_dim(q, s0, Q_BLOCK, axis=1)
        qp = lax.dynamic_slice_in_dim(pos, s0, Q_BLOCK)
        return stick_breaking(qb, k, v, qp, pos)

    out = lax.map(blk, jnp.arange(L // Q_BLOCK))
    return jnp.moveaxis(out, 0, 1).reshape(bsz, L, H, d)

def band_attend(q, k, v, q_pos, k_pos, bias_table):
    s = jnp.einsum('bqhd,bkhd->bhqk', q, k).astype(F32) * (q.shape[-1] ** -0.5)
    rel = jnp.clip(q_pos[:, None] - k_pos[None, :], -REL_CLIP, REL_CLIP) + REL_CLIP
    s = s + bias_table.astype(F32)[:, rel][None]
    qc = jnp.floor_divide(q_pos, CHUNK)[:, None]
    kc = jnp.floor_divide(k_pos, CHUNK)[None, :]
    mask = (k_pos >= 0)[None, :] & (kc <= qc) & (kc >= qc - BAND_CHUNKS)
    p = jax.nn.softmax(jnp.where(mask, s, -1e30), axis=-1)
    return jnp.einsum('bhqk,bkhd->bqhd', p, v.astype(F32))

def band_prompt(q, k, v, bias_table):
    bsz, L, H, d = q.shape
    pad = jnp.zeros((bsz, BAND_WINDOW, H, d), k.dtype)
    kp = jnp.concatenate([pad, k], axis=1)
    vp = jnp.concatenate([pad, v], axis=1)
    pos = jnp.arange(L, dtype=jnp.int32)
    kpos = jnp.arange(-BAND_WINDOW, L, dtype=jnp.int32)
    span = BAND_WINDOW + CHUNK

    def one(i):
        s0 = i * CHUNK
        return band_attend(lax.dynamic_slice_in_dim(q, s0, CHUNK, axis=1),
                           lax.dynamic_slice_in_dim(kp, s0, span, axis=1),
                           lax.dynamic_slice_in_dim(vp, s0, span, axis=1),
                           lax.dynamic_slice_in_dim(pos, s0, CHUNK),
                           lax.dynamic_slice_in_dim(kpos, s0, span), bias_table)

    out = lax.map(one, jnp.arange(L // CHUNK))
    return jnp.moveaxis(out, 0, 1).reshape(bsz, L, H, d)

def causal_conv(u, buf, w, b):
    L = u.shape[1]
    full = jnp.concatenate([buf, u], axis=1)
    acc = b.astype(F32) + sum(full[:, i:i + L].astype(F32) * w[i].astype(F32) for i in range(SSD_CONV))
    return jax.nn.silu(acc).astype(u.dtype), full[:, L:]

def ssd(x, dt, a, bm, cm, state0):
    bsz, L, H, P = x.shape
    G, N = bm.shape[2], bm.shape[3]
    R = H // G
    c = min(CHUNK, L)
    n = L // c
    xd = x.astype(F32) * dt[..., None]
    da = dt * a

    def chunks(t):
        return jnp.moveaxis(t.astype(F32).reshape((bsz, n, c) + t.shape[2:]), 1, 0)

    causal = jnp.tril(jnp.ones((c, c), dtype=bool))[None, :, :, None]

    def step(S, inp):
        xi, dai, bi, ci = inp
        cum = jnp.cumsum(dai, axis=1)
        seg = jnp.exp(jnp.where(causal, cum[:, :, None, :] - cum[:, None, :, :], -jnp.inf))
        cb = jnp.einsum('bign,bjgn->bgij', ci, bi)
        xg = xi.reshape(bsz, c, G, R, P)
        y = jnp.einsum('bgij,bijgr,bjgrp->bigrp', cb, seg.reshape(bsz, c, c, G, R), xg)
        y = y + jnp.einsum('bign,bgrpn->bigrp', ci, S.reshape(bsz, G, R, P, N)) * jnp.exp(cum).reshape(bsz, c, G, R)[..., None]
        last = cum[:, -1]
        w_rem = jnp.exp(last[:, None, :] - cum).reshape(bsz, c, G, R)
        S = S * jnp.exp(last)[:, :, None, None] + jnp.einsum('bjgrp,bjgn->bgrpn', xg * w_rem[..., None], bi).reshape(bsz, H, P, N)
        return S, y.reshape(bsz, c, H, P)

    S, y = lax.scan(step, state0.astype(F32), (chunks(xd), chunks(da), chunks(bm), chunks(cm)))
    return jnp.moveaxis(y, 0, 1).reshape(bsz, L, H, P), S

def ab_mixer(h, pos, w_in, ret_gain, w_out, ret_state, sb_past):
    bsz, L, _ = h.shape
    o1 = RET_QK_W
    o2 = o1 + RET_QK_W
    o3 = o2 + RET_V_W
    o4 = o3 + RET_V_W
    o5 = o4 + SB_W
    o6 = o5 + SB_W
    rq, rk, rv, rg, sq, sk, sv = jnp.split(h @ w_in, [o1, o2, o3, o4, o5, o6], axis=-1)
    rq = rotary(rq.reshape(bsz, L, RET_HEADS, RET_DK), pos) * (RET_DK ** -0.5)
    rk = rotary(rk.reshape(bsz, L, RET_HEADS, RET_DK), pos)
    rv = rv.reshape(bsz, L, RET_HEADS, RET_DV)
    if ret_state is None:
        ret_state = jnp.zeros((bsz, RET_HEADS, RET_DK, RET_DV), F32)
    ro, ret_new = retention(rq, rk, rv, ret_state)
    ro = ro * lax.rsqrt(jnp.mean(ro * ro, axis=-1, keepdims=True) + EPS)
    ro = ro.reshape(bsz, L, RET_V_W) * ret_gain.astype(F32) * jax.nn.silu(rg.astype(F32))
    sq = sq.reshape(bsz, L, SB_HEADS, SB_DH)
    sk = sk.reshape(bsz, L, SB_HEADS, SB_DH)
    sv = sv.reshape(bsz, L, SB_HEADS, SB_DH)
    if sb_past is None:
        so = stick_breaking_blocks(sq, sk, sv)
    else:
        ck, cv = sb_past
        past = ck.shape[1]
        k_all = jnp.concatenate([ck.astype(sk.dtype), sk], axis=1)
        v_all = jnp.concatenate([cv.astype(sv.dtype), sv], axis=1)
        so = stick_breaking(sq, k_all, v_all, pos, jnp.arange(past + L, dtype=jnp.int32))
    mix = jnp.concatenate([ro.astype(h.dtype), so.reshape(bsz, L, SB_W).astype(h.dtype)], axis=-1)
    return mix @ w_out, ret_new.astype(h.dtype), sk, sv

def cd_mixer(h, pos, w_in, rel_bias, conv_w, conv_b, dt_bias, a_log, d_skip, ssd_gain, w_out,
             band_past, ssm_state, conv_buf):
    bsz, L, _ = h.shape
    o1 = BAND_W
    o2 = 2 * BAND_W
    o3 = 3 * BAND_W
    o4 = o3 + SSD_INNER
    o5 = o4 + SSD_CONV_DIM
    bq, bk, bv, z, xbc, dt = jnp.split(h @ w_in, [o1, o2, o3, o4, o5], axis=-1)
    bq = bq.reshape(bsz, L, BAND_HEADS, BAND_DH)
    bk = bk.reshape(bsz, L, BAND_HEADS, BAND_DH)
    bv = bv.reshape(bsz, L, BAND_HEADS, BAND_DH)
    if band_past is None:
        bo = band_prompt(bq, bk, bv, rel_bias)
        keep = min(BAND_WINDOW, L)
        new_k, new_v = bk[:, L - keep:], bv[:, L - keep:]
    else:
        ck, cv = band_past
        wlen = ck.shape[1]
        k_all = jnp.concatenate([ck.astype(bk.dtype), bk], axis=1)
        v_all = jnp.concatenate([cv.astype(bv.dtype), bv], axis=1)
        k_pos = jnp.concatenate([pos[0] - wlen + jnp.arange(wlen, dtype=jnp.int32), pos])
        bo = band_attend(bq, k_all, v_all, pos, k_pos, rel_bias)
        new_k, new_v = bk, bv
    if conv_buf is None:
        conv_buf = jnp.zeros((bsz, SSD_CONV - 1, SSD_CONV_DIM), xbc.dtype)
    if ssm_state is None:
        ssm_state = jnp.zeros((bsz, SSD_HEADS, SSD_P, SSD_N), F32)
    xbc, conv_new = causal_conv(xbc, conv_buf.astype(xbc.dtype), conv_w, conv_b)
    xs, bm, cm = jnp.split(xbc, [SSD_INNER, SSD_INNER + SSD_GROUPS * SSD_N], axis=-1)
    xs = xs.reshape(bsz, L, SSD_HEADS, SSD_P)
    dt = jax.nn.softplus(dt.astype(F32) + dt_bias.astype(F32))
    a = -jnp.exp(a_log.astype(F32))
    y, ssm_new = ssd(xs, dt, a, bm.reshape(bsz, L, SSD_GROUPS, SSD_N), cm.reshape(bsz, L, SSD_GROUPS, SSD_N), ssm_state)
    y = y + d_skip.astype(F32)[:, None] * xs.astype(F32)
    y = rms_norm(y.reshape(bsz, L, SSD_INNER) * jax.nn.silu(z.astype(F32)), ssd_gain)
    mix = jnp.concatenate([bo.reshape(bsz, L, BAND_W).astype(h.dtype), y.astype(h.dtype)], axis=-1)
    return mix @ w_out, new_k, new_v, ssm_new.astype(h.dtype), conv_new

def trunk(x, pos, weights, past):
    (norm_g, ffn_w_in, ffn_w_out, final_g, w_in_ab, ret_gain, w_out_ab, w_in_cd, rel_bias,
     conv_w, conv_b, dt_bias, a_log, d_skip, ssd_gain, w_out_cd) = weights
    outs = ([], [], [], [], [], [], [])
    for l in range(DEPTH):
        j = l // 2
        x = x + 0.5 * swiglu(rms_norm(x, norm_g[l, 0]), ffn_w_in[l, 0], ffn_w_out[l, 0])
        h = rms_norm(x, norm_g[l, 1])
        if l % 2 == 0:
            ret0 = None if past is None else past[0][j]
            sbp = None if past is None else (past[1][j], past[2][j])
            y, r, k, v = ab_mixer(h, pos, w_in_ab[j], ret_gain[j], w_out_ab[j], ret0, sbp)
            outs[0].append(r)
            outs[1].append(k)
            outs[2].append(v)
        else:
            bp = None if past is None else (past[3][j], past[4][j])
            s0 = None if past is None else past[5][j]
            c0 = None if past is None else past[6][j]
            y, k, v, s, cb = cd_mixer(h, pos, w_in_cd[j], rel_bias[j], conv_w[j], conv_b[j], dt_bias[j],
                                      a_log[j], d_skip[j], ssd_gain[j], w_out_cd[j], bp, s0, c0)
            outs[3].append(k)
            outs[4].append(v)
            outs[5].append(s)
            outs[6].append(cb)
        x = x + y
        x = x + 0.5 * swiglu(rms_norm(x, norm_g[l, 2]), ffn_w_in[l, 1], ffn_w_out[l, 1])
    return rms_norm(x, final_g), tuple(jnp.stack(o) for o in outs)

def setup_inputs(seed: int = 0) -> dict:
    key = jax.random.key(seed)
    ks = jax.random.split(key, 32)

    def nrm(k, shape, s):
        return jax.random.normal(k, shape, F32) * s

    band_rows = min(BAND_WINDOW, PAST_LEN)
    dt0 = jnp.exp(jax.random.uniform(ks[20], (N_CD, SSD_HEADS), F32) * (math.log(0.1) - math.log(1e-3)) + math.log(1e-3))
    dt_bias = dt0 + jnp.log(-jnp.expm1(-dt0))
    a_log = jnp.log(jax.random.uniform(ks[21], (N_CD, SSD_HEADS), F32, minval=1.0, maxval=16.0))
    return {
        'x_prompt': nrm(ks[0], (BATCH, SEQ, D_MODEL), 1.0),
        'x_sample': nrm(ks[1], (DEC_BATCH, DEC_SEQ, D_MODEL), 1.0),
        'state_ret': nrm(ks[2], (N_AB, DEC_BATCH, RET_HEADS, RET_DK, RET_DV), 0.5),
        'cache_sb_k': nrm(ks[3], (N_AB, DEC_BATCH, PAST_LEN, SB_HEADS, SB_DH), 1.0),
        'cache_sb_v': nrm(ks[4], (N_AB, DEC_BATCH, PAST_LEN, SB_HEADS, SB_DH), 1.0),
        'cache_band_k': nrm(ks[5], (N_CD, DEC_BATCH, band_rows, BAND_HEADS, BAND_DH), 1.0),
        'cache_band_v': nrm(ks[6], (N_CD, DEC_BATCH, band_rows, BAND_HEADS, BAND_DH), 1.0),
        'state_ssm': nrm(ks[7], (N_CD, DEC_BATCH, SSD_HEADS, SSD_P, SSD_N), 0.1),
        'state_conv': nrm(ks[8], (N_CD, DEC_BATCH, SSD_CONV - 1, SSD_CONV_DIM), 1.0),
        'norm_g': 1.0 + nrm(ks[9], (DEPTH, 3, D_MODEL), 0.02),
        'ffn_w_in': nrm(ks[10], (DEPTH, 2, D_MODEL, 2 * D_FF), D_MODEL ** -0.5),
        'ffn_w_out': nrm(ks[11], (DEPTH, 2, D_FF, D_MODEL), D_FF ** -0.5),
        'final_g': 1.0 + nrm(ks[12], (D_MODEL,), 0.02),
        'w_in_ab': nrm(ks[13], (N_AB, D_MODEL, AB_IN), D_MODEL ** -0.5),
        'ret_gain': 1.0 + nrm(ks[14], (N_AB, RET_V_W), 0.02),
        'w_out_ab': nrm(ks[15], (N_AB, AB_OUT, D_MODEL), AB_OUT ** -0.5),
        'w_in_cd': nrm(ks[16], (N_CD, D_MODEL, CD_IN), D_MODEL ** -0.5),
        'rel_bias': nrm(ks[17], (N_CD, BAND_HEADS, 2 * REL_CLIP + 1), 0.2),
        'conv_w': nrm(ks[18], (N_CD, SSD_CONV, SSD_CONV_DIM), SSD_CONV ** -0.5),
        'conv_b': nrm(ks[19], (N_CD, SSD_CONV_DIM), 0.01),
        'dt_bias': dt_bias,
        'a_log': a_log,
        'd_skip': 1.0 + nrm(ks[22], (N_CD, SSD_HEADS), 0.1),
        'ssd_gain': 1.0 + nrm(ks[23], (N_CD, SSD_INNER), 0.02),
        'w_out_cd': nrm(ks[24], (N_CD, CD_OUT, D_MODEL), CD_OUT ** -0.5),
    }

def reference(x_prompt, x_sample, state_ret, cache_sb_k, cache_sb_v, cache_band_k, cache_band_v,
              state_ssm, state_conv, norm_g, ffn_w_in, ffn_w_out, final_g, w_in_ab, ret_gain, w_out_ab,
              w_in_cd, rel_bias, conv_w, conv_b, dt_bias, a_log, d_skip, ssd_gain, w_out_cd):
    weights = (norm_g, ffn_w_in, ffn_w_out, final_g, w_in_ab, ret_gain, w_out_ab, w_in_cd, rel_bias,
               conv_w, conv_b, dt_bias, a_log, d_skip, ssd_gain, w_out_cd)
    pos_p = jnp.arange(x_prompt.shape[1], dtype=jnp.int32)
    y_prompt, (p_ret, p_sb_k, p_sb_v, p_band_k, p_band_v, p_ssm, p_conv) = trunk(x_prompt, pos_p, weights, None)
    past_len = cache_sb_k.shape[2]
    pos_s = past_len + jnp.arange(x_sample.shape[1], dtype=jnp.int32)
    past = (state_ret, cache_sb_k, cache_sb_v, cache_band_k, cache_band_v, state_ssm, state_conv)
    y_sample, (s_ret, s_sb_k, s_sb_v, s_band_k, s_band_v, s_ssm, s_conv) = trunk(x_sample, pos_s, weights, past)
    return (y_prompt, y_sample, p_ret, p_sb_k, p_sb_v, p_band_k, p_band_v, p_ssm, p_conv,
            s_ret, s_sb_k, s_sb_v, s_band_k, s_band_v, s_ssm, s_conv)


_drawn_inputs = setup_inputs


def setup_inputs(seed=0):
    import zlib

    import numpy as np

    out = dict(_drawn_inputs(seed))
    spreads = {}
    factors = {'final_g': 8.341,
     'ret_gain': 4.045,
     'rel_bias': 14.655,
     'conv_b': 3.604,
     'ssd_gain': 19.908,
     'cache_band_k': 3.566}
    for name, (base, spread) in spreads.items():
        noise = np.random.default_rng([zlib.crc32(name.encode()), seed]).standard_normal(out[name].shape)
        drawn = base * np.exp(spread * noise) if base else spread * noise
        out[name] = jnp.asarray(drawn.astype(out[name].dtype))
    for name, factor in factors.items():
        out[name] = (out[name] * factor).astype(out[name].dtype)
    return out
```

```python
from contextlib import ExitStack

import numpy as np

import concourse.bass as bass
from concourse import mybir

ALU = mybir.AluOpType
ACT = mybir.ActivationFunctionType
AXX = mybir.AxisListType.X
F32 = mybir.dt.float32
F32R = mybir.dt.float32r

P = 128
LP, LS = 512, 32
T = LP + LS
HT = T // 2
D = 1024
DC = D // P
FF = 2816
FC = FF // P
G = 2
GC = FC // G
PAST = 256
EPS = 1e-6
NEG = -1e30
RET_H, RET_DK, RET_DV = 4, 64, 128
SB_H, DH = 8, 64
SSD_H, SSD_P, SSD_G, SSD_N = 8, 64, 2, 128
TAPS = 4
TILES = LP // P
NORMS = 7

OFF = {0: 0, 1: 512, 3: 896, 2: 1024}
LEN = {j: LP - P * j for j in range(TILES)}
ZW = 1280

C_ID, C_ONE, C_LE, C_GT, C_STRICT, C_NEGT, C_NEG1, C_ROT, C_MASKNEG, C_KDEC, C_QDEC = (
    [128 * i for i in range(9)] + [1152, 1152 + 20])
NCONST = C_QDEC + 64
A_DEC, A_COS, A_SIN = 0, 4 * LP, 4 * LP + T
NTAB = A_SIN + T
P_NORM, P_FINAL, P_RET, P_SSD, P_CW, P_CB, P_DTB, P_ALOG, P_DSKIP, P_EPS = (
    0, 48, 56, 60, 64, 96, 104, 105, 106, 114)
NPAR = 116


def tables():
    c = np.zeros((P, NCONST), np.float64)
    r = np.arange(P)
    row, col = r[:, None], r[None, :]
    c[:, C_ID:C_ID + P] = row == col
    c[:, C_ONE:C_ONE + P] = 1
    c[:, C_LE:C_LE + P] = row <= col
    c[:, C_GT:C_GT + P] = row > col
    c[:, C_STRICT:C_STRICT + P] = row < col
    c[:, C_NEGT:C_NEGT + P] = -(row >= col).astype(float)
    c[:, C_NEG1:C_NEG1 + P] = -1
    same = row // 64 == col // 64
    m = col % 64
    c[:, C_ROT:C_ROT + P] = same * ((m < 32) * (row % 64 == m + 32) * -1.0 + (m >= 32) * (row % 64 == m - 32) * 1.0)
    c[:, C_MASKNEG:C_MASKNEG + P] = np.where(row < col, 0.0, NEG)
    lg = np.log1p(-np.exp2(-5.0 - np.arange(RET_H)))
    for h in range(RET_H):
        for t in range(TILES):
            c[:, C_KDEC + 4 * t + h] = np.exp(lg[h] * (LP - 1 - P * t - r))
        c[:LS, C_KDEC + 4 * TILES + h] = np.exp(lg[h] * (LS - 1 - r[:LS]))
        half = slice(64 * (h % 2), 64 * (h % 2) + 64)
        at = C_QDEC + LS * (h // 2)
        c[half, at:at + LS] = np.exp(lg[h] * (np.arange(LS) + 1.0))[None] * RET_DK ** -0.5
    a = np.zeros((P, NTAB), np.float64)
    i = np.arange(LP)[None, :]
    for h in range(RET_H):
        a[:, A_DEC + LP * h:A_DEC + LP * (h + 1)] = np.where(
            i >= row, np.exp(lg[h] * np.maximum(i - row, 0)), 0.0) * RET_DK ** -0.5
    pos = np.concatenate([np.arange(LP), PAST + np.arange(LS)]).astype(np.float32)
    inv = np.power(np.float32(10000.0), -np.arange(32, dtype=np.float32) / np.float32(32))
    ang = (pos[None, :] * inv[r % 32][:, None].astype(np.float32)).astype(np.float32).astype(np.float64)
    a[:, A_COS:A_COS + T] = np.cos(ang)
    a[:, A_SIN:A_SIN + T] = np.sin(ang)
    return c.astype(np.float32), a.astype(np.float32), np.exp(lg * LS)


def trunk(nc, ins, outs, ret_cdec):
    with ExitStack() as ctx:
        at = [(nc.sbuf_base + 63) // 64 * 64]

        def place(name, shape, dt, offset):
            return nc.alloc_sbuf_tensor_at(name, [P] + shape, dt, offset=offset)

        def sb(name, shape, dt=F32):
            size = 4 * int(np.prod(shape))
            t = place(name, shape, dt, at[0])
            at[0] += (size + 31) // 32 * 32
            return t

        x = sb("x", [DC, T])
        u_at = at[0]
        u = sb("u", [DC, 2, T], F32R)
        a_at = at[0]
        a = sb("a", [GC, 2, T], F32R)
        wh = sb("wh", [2, GC * P], F32R)
        wl = sb("wl", [2, GC * P], F32R)
        wraw = sb("wraw", [2, 2 * GC * P])
        const = sb("const", [NCONST])
        par = sb("par", [NPAR])
        tab_at = at[0]
        bt = sb("bt", [SB_H, 512])
        tab = place("tab", [NTAB], F32, tab_at)
        rms = sb("rms", [T])
        rstd = sb("rstd", [T])
        ssum = sb("ssum", [T])
        sq = sb("sq", [2, T])
        tg = sb("tg", [2, T])
        sil = sb("sil", [T])
        free_at = at[0]
        SC = DC * 0 + 2 * T * 4

        sq_t = place("sq_t", [4, T], F32, free_at)
        sk_t = place("sk_t", [4, T], F32, free_at + 8704)
        sv_n = place("sv_n", [5, 512], F32, free_at + 17408)
        kc_t = place("kc_t", [4, PAST], F32, a_at + 4 * SC + 17408)
        vc_n = place("vc_n", [2, 512], F32, a_at + 4 * SC + 21504)
        s0 = place("s0", [2, P], F32, a_at + 4 * SC + 28672)
        qs = place("qs", [2, 2, LS], F32, free_at + 27648)
        sqz = place("sqz", [4, 2, LS], F32, a_at + 4 * SC + 27648)
        ab_end = free_at + 28160
        rqk = place("rqk", [4, T], F32, a_at + 4 * SC)
        rg = place("rg", [4, T], F32, a_at + 4 * SC + 8704)
        rv_n = place("rv_n", [5, 512], F32, a_at + 4 * SC + 17408)
        att = place("att", [2, ZW + LS], F32, u_at)
        kd = place("kd", [5, 256], F32, u_at + 10496)
        ro = place("ro", [4, T], F32, a_at)
        rsq = place("rsq", [4, T], F32, a_at + 8704)
        se = place("se", [3, ZW], F32, u_at)
        sps = [place("sps0", [2, ZW], F32R, u_at + 15616), place("sps1", [2, ZW], F32R, tab_at)]
        cr = place("cr", [4, P], F32R, u_at + 25856)
        CR_NEGT, CR_NEG1, CR_ID, CR_MASK = range(4)
        bq_t = place("bq_t", [4, T], F32, free_at)
        bk_t = place("bk_t", [4, T], F32, free_at + 8704)
        bv_n = place("bv_n", [5, 512], F32, free_at + 17408)
        bc_t = place("bc_t", [4, T], F32, a_at + 2 * SC)
        dtn = place("dtn", [5, 40], F32, free_at + 27648)
        cs = place("cs", [DC, 3], F32, a_at + 4 * SC + 28480)
        cnew = place("cnew", [DC, 2, 3], F32, a_at + 4 * SC + 28576)
        cd_end = free_at + 28448
        bqz = place("bqz", [4, 2, LS], F32, u_at + 32768)
        zs = place("zs", [4, T], F32, a_at + 4 * SC)
        xs_n = place("xs_n", [5, 512], F32, a_at + 4 * SC + 8704)
        b_n = place("b_n", [5, 256], F32, a_at + 4 * SC + 18944)
        xpad = place("xpad", [2, 550], F32, a_at + 4 * SC + 24064)
        cacc = place("cacc", [547], F32, a_at)
        dtda = place("dtda", [T], F32, a_at + SC)
        dtl = place("dtl", [T], F32, a_at + SC + 2176)
        hl = place("hl", [SSD_H, P], F32, u_at)
        seg = place("seg", [SSD_H, P], F32, u_at + 4096)
        cbm = place("cbm", [SSD_G, P], F32, u_at + 8192)
        xd = place("xd", [512], F32, u_at + 9216)
        xw = place("xw", [512], F32, u_at + 11264)
        yn = place("yn", [512], F32, u_at + 13312)
        yt = place("yt", [512], F32, u_at + 15360)
        eg = place("eg", [24], F32, u_at + 17408)
        sst = place("sst", [2, 512], F32, u_at + 17536)
        yz = place("yz", [4, T], F32, u_at + 21632)
        ea = place("ea", [1], F32, u_at + 30336)
        yq = place("yq", [4, T], F32, u_at)
        yout = place("yout", [DC, T], F32, a_at)
        pr = place("pr", [3, 512], F32, u_at)
        pt = place("pt", [2, 512], F32, u_at + 6144)
        on = place("on", [5, 512], F32, u_at + 21632)
        bst = place("bst", [3, 4], F32, u_at + 33792)
        kb_t = place("kb_t", [4, PAST], F32, a_at + 4 * SC + 18944)
        vb_n = place("vb_n", [2, 512], F32, a_at + 4 * SC + 23040)
        assert max(ab_end, cd_end) <= nc.sbuf_usable_end, (ab_end, cd_end, nc.sbuf_usable_end)

        ps = ctx.enter_context(nc.psum_tensor("ps", [P, 8, 512], F32))
        psf = ps[:].rearrange("p b n -> p (b n)")

        def bank(b, lo=0, hi=512, r0=0, r1=P):
            return ps[r0:r1, b, lo:hi]

        def pair(b):
            return ps[:, b:b + 2, 0:HT]

        def halves(ap):
            return ap.rearrange("p (a b) -> p a b", a=2)

        def sem(name):
            return ctx.enter_context(nc.semaphore(name))

        def C(at_, n=P, r0=0, r1=P):
            return const[r0:r1, at_:at_ + n]

        x_loaded = [sem(f"x_loaded{m}") for m in range(DC)]
        par_loaded, const_loaded, tab_loaded = sem("par_loaded"), sem("const_loaded"), sem("tab_loaded")
        cache_loaded, bt_loaded, cdc_loaded = sem("cache_loaded"), sem("bt_loaded"), sem("cdc_loaded")
        raw_loaded = [sem("raw_loaded0"), sem("raw_loaded1")]
        w_high = sem("w_high")
        w_split = [sem("w_split0"), sem("w_split1")]
        prod_done = [sem("prod_done0"), sem("prod_done1")]
        evac = [sem("evac0"), sem("evac1")]
        u_high, u_ready = sem("u_high"), sem("u_ready")
        sq_done, ss_added, ss_total, rms_root, rstd_ready = (
            sem("sq_done"), sem("ss_added"), sem("ss_total"), sem("rms_root"), sem("rstd_ready"))
        sil_done, glu_done, act_high, act_ready = (
            sem("sil_done"), sem("glu_done"), sem("act_high"), sem("act_ready"))
        out_done = sem("out_done")
        y_ready = sem("y_ready")
        dve_step, act_step, pool_step = sem("dve_step"), sem("act_step"), sem("pool_step")
        conv_src, tp_done, tp_free = sem("conv_src"), sem("tp_done"), sem("tp_free")
        rot_src, rot_done, rot_free, rg_ready = sem("rot_src"), sem("rot_done"), sem("rot_free"), sem("rg_ready")
        rs_done, rs_att, ro_done, ro_evac, ro_sq, ro_ss, ro_root, ret_mix, cr_ready = (
            sem("rs_done"), sem("rs_att"), sem("ro_done"), sem("ro_evac"), sem("ro_sq"), sem("ro_ss"),
            sem("ro_root"), sem("ret_mix"), sem("cr_ready"))
        kt_done, kd_ready, st_done, st_ready = sem("kt_done"), sem("kd_ready"), sem("st_done"), sem("st_ready")
        qs_ready, skv_out = sem("qs_ready"), [sem("skv_out0"), sem("skv_out1")]
        z_done, sb_ln, sb_sp, sb_high, cum_done, sb_w, so_done, so_mix = (
            sem("z_done"), sem("sb_ln"), sem("sb_sp"), sem("sb_high"), sem("cum_done"), sem("sb_w"),
            sem("so_done"), sem("so_mix"))
        conv_acc, conv_out, dt_evac, dt_ln, dt_ready, dtn_done, dtn_ready, a_neg = (
            sem("conv_acc"), sem("conv_out"), sem("dt_evac"), sem("dt_ln"), sem("dt_ready"), sem("dtn_done"),
            sem("dtn_ready"), sem("a_neg"))
        z_silu = sem("z_silu")
        g_done, g_exp, cb_done, hl_ready, seg_done, seg_exp, m_ready, xw_ready, y_done, y_sum, yt_done, yz_done = (
            sem("g_done"), sem("g_exp"), sem("cb_done"), sem("hl_ready"), sem("seg_done"), sem("seg_exp"),
            sem("m_ready"), sem("xw_ready"), sem("y_done"), sem("y_sum"), sem("yt_done"), sem("yz_done"))
        s_scaled, sst_ready, sst_loaded, yss_done, y_root, ssd_mix = (
            sem("s_scaled"), sem("sst_ready"), sem("sst_loaded"), sem("yss_done"), sem("y_root"), sem("ssd_mix"))
        bs_done, b_max, b_exp, b_norm, bp_done, bp_copied, bo_done, band_mix, bt_masked = (
            sem("bs_done"), sem("b_max"), sem("b_exp"), sem("b_norm"), sem("bp_done"), sem("bp_copied"),
            sem("bo_done"), sem("band_mix"), sem("bt_masked"))
        y_sq, conv_left, bo_evac, bb_done = sem("y_sq"), sem("conv_left"), sem("bo_evac"), sem("bb_done")

        stages = []
        for f in range(2):
            stages += [(ins["wf_in"][f, 0], GC, DC), (ins["wf_out"][f, 0], DC // 2, GC),
                       (ins["wf_in"][f, 1], GC, DC), (ins["wf_out"][f, 1], DC // 2, GC)]
            if f == 0:
                stages += [(ins["w_ab"], 12, DC), (ins["w_abo"], DC // 2, DC)]
        for f in range(2, 4):
            stages += [(ins["wf_in"][f, 0], GC, DC), (ins["wf_out"][f, 0], DC // 2, GC),
                       (ins["wf_in"][f, 1], GC, DC), (ins["wf_out"][f, 1], DC // 2, GC)]
            if f == 2:
                stages += [(ins["w_cd"], 12, DC), (ins["w_dt"], 1, DC), (ins["w_cdo"], DC // 2, DC)]
        STAGE = {}
        pairs, slot = 0, [0, 0]
        for n, (arr, count, K) in enumerate(stages):
            lone = arr is ins["w_dt"]
            STAGE[n] = (pairs, slot[0], slot[1], count, K, lone)
            pairs += count
            slot = [slot[0] + count, slot[1] + (0 if lone else count)]
        FFN_STAGE = [0, 6, 10, 17]
        AB_IN, AB_OUT, CD_IN, CD_DT, CD_OUT = 4, 5, 14, 15, 16

        def pairs_loop(eng, n, body):
            first, _, _, count, _, _ = STAGE[n]
            if count >= 2:
                with eng.Fori(0, count // 2) as i:
                    for j in range(2):
                        body(2 * i + j, (first + j) % 2, i, j)
            if count % 2:
                body(count - 1, (first + count - 1) % 2, count // 2, 0)

        ctx.enter_context(nc.allow_non_contiguous_dma(reason="small tables"))
        block = ctx.enter_context(nc.Block())

        @block.sync
        def _(sp):
            for n, (arr, count, K) in enumerate(stages):
                first, c0, c1, _, _, lone = STAGE[n]
                width = (1 if lone else 2) * K * P

                def load(i, par_, *_):
                    sp.dma_start(wraw[:, par_, 0:width], arr[i]).then_inc(raw_loaded[par_], 16)

                def load_after(i, par_, *_):
                    sp.wait_ge(w_split[1], c1 + i - 1)
                    load(i, par_)

                if n == 0:
                    load(0, 0)
                    load(1, 1)
                    with sp.Fori(1, count // 2) as it:
                        for j in range(2):
                            load_after(2 * it + j, j)
                    load_after(count - 1, (count - 1) % 2)
                elif n == CD_OUT:
                    for i in range(count):
                        if i == 1:
                            sp.wait_ge(w_split[0], c0)
                        sp.wait_ge(w_split[1], c1 + max(i - 1, 0))
                        load(i, (first + i) % 2)
                else:
                    pairs_loop(sp, n, load_after)

        @block.gpsimd
        def _(pool):
            high = ctx.enter_context(pool.register("highs"))
            pool.reg_mov(high, 0)
            for n, (arr, count, K) in enumerate(stages):
                first, c0, c1, _, _, lone = STAGE[n]
                per = 1 if lone else 2

                def split(i, par_, it, j):
                    pool.wait_ge(raw_loaded[par_], 16 * ((first + j) // 2 + 1 + it))
                    for s in range(per):
                        if not isinstance(i, int) or (c0, c1)[s] + i:
                            pool.wait_ge(prod_done[s], (c0, c1)[s] + i)
                        pool.reg_add(high, high, 1)
                        raw = wraw[:, par_, s * K * P:(s + 1) * K * P]
                        nc.gpsimd.tensor_scalar(wh[:, s, 0:K * P], raw, 1.0, 1.0, ALU.mult,
                                                ALU.mult).then_inc(w_high, 1)
                        pool.wait_ge(w_high, pool.snap(high))
                        nc.gpsimd.tensor_tensor(wl[:, s, 0:K * P], raw, wh[:, s, 0:K * P].bitcast(F32),
                                                ALU.subtract).then_inc(w_split[s], 1)

                if n == 0:
                    split(0, 0, 0, 0)
                    split(1, 1, 0, 1)
                    with pool.Fori(1, count // 2) as it:
                        for j in range(2):
                            split(2 * it + j, j, it, j)
                    split(count - 1, (count - 1) % 2, count // 2, 0)
                else:
                    pairs_loop(pool, n, split)

        @block.tensor
        def _(pe):
            def product(s, c, K, act_t, ready, base, order=None, extra=None):
                pe.wait_ge(w_split[s], c + 1)
                if not isinstance(c, int) or c:
                    pe.wait_ge(evac[s], c)
                for k in range(K):
                    if ready is not None:
                        pe.wait_ge(ready, base + k + 1)
                    for w, parts in ((wh, (0, 1)), (wl, (0,))):
                        for part in parts:
                            for half in range(2):
                                last = nc.tensor.matmul(
                                    bank(2 * s + half, 0, HT), w[:, s, k * P:(k + 1) * P],
                                    act_t[:, k, part, half * HT:(half + 1) * HT],
                                    start=(k == 0 and w is wh and part == 0), stop=(k == K - 1 and w is wl))
                last.then_inc(prod_done[s], 1)

            def sum_squares(n):
                pe.wait_ge(ss_added, (DC - 1) * (n + 1))
                if n == 0:
                    pe.wait_ge(const_loaded, 16)
                if n:
                    pe.wait_ge(rms_root, n)
                for half in range(2):
                    last = nc.tensor.matmul(bank(4 + half, 0, HT), C(C_ONE), ssum[:, half * HT:(half + 1) * HT],
                                            start=True, stop=True)
                last.then_inc(ss_total, 1)

            def run(stage, act_t, ready, base, lo=0, hi=None, body=None):
                _, c0, c1, count, K, _ = STAGE[stage]
                hi = count if hi is None else hi
                if hi - lo == 1:
                    product(0, c0 + lo, K, act_t, ready, base)
                    product(1, c1 + lo, K, act_t, ready, base)
                    if body:
                        body(0)
                    return
                with pe.Fori(lo, hi) as i:
                    product(0, c0 + i, K, act_t, ready, base)
                    product(1, c1 + i, K, act_t, ready, base)
                    if body:
                        body(i - lo)

            def first_pair(stage, n):
                _, c0, c1, _, K, _ = STAGE[stage]
                product(0, c0, K, u, u_ready, DC * n)
                sum_squares(n)
                product(1, c1, K, u, u_ready, DC * n)

            def ffn(f, n):
                st = FFN_STAGE[f]
                first_pair(st, n)
                run(st, u, None, 0, 1)
                run(st + 1, a, act_ready, FC * f)
                run(st + 2, u, None, 0)
                run(st + 3, a, act_ready, FC * f + GC)

            def turn_chunk(src, c, source, value):
                pe.wait_ge(source, value)
                pe.wait_ge(tp_free, c)
                for t in range(TILES):
                    nc.tensor.transpose(bank(6, t * P, (t + 1) * P), src[:, t * P:(t + 1) * P], C(C_ID))
                nc.tensor.transpose(bank(7, 0, P, 0, LS), src[:, LP:T], C(C_ID)).then_inc(tp_done, 1)

            ffn(0, 0)
            first_pair(AB_IN, 1)
            ca = STAGE[AB_IN][1:3]
            for s in range(2):
                turn_chunk(tg[:, s, :], s, evac[s], ca[s] + 1)
            run(AB_IN, u, None, 0, 1, 4, body=lambda i: [
                turn_chunk(tg[:, s, :], 2 * (i + 1) + s, evac[s], ca[s] + i + 2) for s in range(2)])

            def rotate(i):
                for s in range(2):
                    pe.wait_ge(rot_src, 2 * i + s + 1)
                    pe.wait_ge(rot_free, 2 * i + s)
                    for half in range(2):
                        last = nc.tensor.matmul(bank(4 + half, 0, HT), C(C_ROT),
                                                tg[:, s, half * HT:(half + 1) * HT], start=True, stop=True)
                    last.then_inc(rot_done, 1)
            pe.wait_ge(rms_root, 2)
            run(AB_IN, u, None, 0, 4, 6, body=rotate)
            run(AB_IN, u, None, 0, 6, 12)
            _, c0, c1, count, _, _ = STAGE[AB_IN]
            pe.wait_ge(evac[0], c0 + count)
            pe.wait_ge(evac[1], c1 + count)
            pe.wait_ge(rot_free, 4)
            pe.wait_ge(tp_free, 8)

            for c in range(2):
                pe.wait_ge(kd_ready, 2 * c)
                for t in range(TILES):
                    nc.tensor.transpose(bank(6, t * P, (t + 1) * P), rqk[:, 2 + c, t * P:(t + 1) * P], C(C_ID))
                nc.tensor.transpose(bank(7, 0, P, 0, LS), rqk[:, 2 + c, LP:T], C(C_ID)).then_inc(kt_done, 1)

            def ret_scores(h):
                c, b = h // 2, 64 * (h % 2)
                B = 3 * (h % 2)
                if h >= 2:
                    pe.wait_ge(rs_att, h - 1)
                base = 512 * B
                for j in (0, 1, 3, 2):
                    nc.tensor.matmul(psf[:, base + OFF[j]:base + OFF[j] + LEN[j]],
                                     rqk[b:b + 64, 2 + c, j * P:(j + 1) * P], rqk[b:b + 64, c, j * P:LP],
                                     start=(j != 3), stop=True, skip_group_check=True)
                nc.tensor.matmul(psf[0:LS, base + ZW:base + ZW + LS], rqk[b:b + 64, 2 + c, LP:T],
                                 rqk[b:b + 64, c, LP:T], start=False, stop=True,
                                 skip_group_check=True).then_inc(rs_done, 1)

            def ret_out(h):
                c, b = h // 2, 64 * (h % 2)
                pe.wait_ge(rs_att, h + 1)
                pe.wait_ge(ro_evac, 2 * h)
                A = att[:, h % 2, :]
                for j in range(TILES):
                    nc.tensor.matmul(bank(6, j * P, 512), rv_n[:, j, h * P:(h + 1) * P],
                                     A[:, OFF[j]:OFF[j] + LEN[j]], start=(j == 0), stop=(j == TILES - 1))
                nc.tensor.matmul(bank(7, 0, LS), rv_n[0:LS, 4, h * P:(h + 1) * P], A[0:LS, ZW:ZW + LS],
                                 start=True, stop=False)
                nc.tensor.matmul(bank(7, 0, LS), s0[:, c, :], qs[:, c, h % 2, :],
                                 start=False, stop=True).then_inc(ro_done, 1)

            pe.wait_ge(cache_loaded, 16)
            pe.wait_ge(kd_ready, 4)
            pe.wait_ge(qs_ready, 1)
            ret_scores(0)
            for h in range(RET_H):
                if h + 1 < RET_H:
                    ret_scores(h + 1)
                ret_out(h)
            pe.wait_ge(ro_evac, 2 * RET_H)
            for h in range(RET_H):
                pe.wait_ge(ro_sq, h + 1)
                for half in range(2):
                    last = nc.tensor.matmul(bank(2 * h + half, 0, HT), C(C_ONE),
                                            rsq[:, h, half * HT:(half + 1) * HT], start=True, stop=True)
                last.then_inc(ro_ss, 1)
            pe.wait_ge(ro_root, 1)
            for h in range(RET_H):
                c, b = h // 2, 64 * (h % 2)
                for j in range(TILES):
                    nc.tensor.matmul(bank(0, c * P, (c + 1) * P, b, b + 64), kd[:, j, h * 64:(h + 1) * 64],
                                     rv_n[:, j, h * P:(h + 1) * P], start=(j == 0), stop=(j == TILES - 1),
                                     skip_group_check=True)
                last = nc.tensor.matmul(bank(1, c * P, (c + 1) * P, b, b + 64), kd[0:LS, 4, h * 64:(h + 1) * 64],
                                        rv_n[0:LS, 4, h * P:(h + 1) * P], start=True, stop=True,
                                        skip_group_check=True)
            last.then_inc(st_done, 1)

            def stick_z(h):
                B = 512 * 3 * (h % 2)
                if h >= 2:
                    pe.wait_ge(sb_w, h - 1)
                if h < SB_H:
                    c, b = h // 2, 64 * (h % 2)
                    for j in (0, 1, 3, 2):
                        last = nc.tensor.matmul(psf[:, B + OFF[j]:B + OFF[j] + LEN[j]],
                                                sk_t[b:b + 64, c, j * P:(j + 1) * P], sq_t[b:b + 64, c, j * P:LP],
                                                start=(j != 3), stop=False, skip_group_check=True)
                else:
                    pe.wait_ge(cache_loaded, 48)
                    for c in range(4):
                        for kt in range(2):
                            at_ = B + 256 * kt + 2 * LS * c
                            nc.tensor.matmul(psf[:, at_:at_ + 2 * LS], kc_t[:, c, kt * P:(kt + 1) * P],
                                             sqz[:, c, :, :], start=(c == 0 and kt == 0), stop=False,
                                             skip_group_check=True)
                        at_ = B + 512 + 2 * LS * c
                        last = nc.tensor.matmul(psf[0:LS, at_:at_ + 2 * LS], sk_t[:, c, LP:T],
                                                sqz[:, c, :, :], start=(c == 0), stop=False,
                                                skip_group_check=True)
                last.then_inc(z_done, 1)

            def stick_cum(h):
                B = 512 * 3 * (h % 2)
                S = se[:, h % 3, :]
                pe.wait_ge(sb_sp, h + 1)
                if h < SB_H:
                    for j in range(TILES):
                        o = B + OFF[j]
                        for part in range(2):
                            S = sps[h % 2][:, part, :]
                            nc.tensor.matmul(psf[:, o:o + LEN[j]], cr[:, CR_NEGT, :], S[:, OFF[j]:OFF[j] + LEN[j]],
                                             start=False, stop=False, skip_group_check=True)
                            for jj in range(j + 1, TILES):
                                nc.tensor.matmul(psf[:, o + P * (jj - j):o + LEN[j]], cr[:, CR_NEG1, :],
                                                 S[:, OFF[jj]:OFF[jj] + LEN[jj]], start=False, stop=False,
                                                 skip_group_check=True)
                        last = nc.tensor.matmul(psf[:, o:o + P], cr[:, CR_ID, :], cr[:, CR_MASK, :], start=False,
                                                stop=True, skip_group_check=True)
                else:
                    for kt in range(3):
                        n = P if kt < 2 else LS
                        o = psf[0:n, B + 256 * kt:B + 256 * (kt + 1)]
                        nc.tensor.matmul(o, C(C_NEGT, n, 0, n), S[0:n, 256 * kt:256 * (kt + 1)], start=False,
                                         stop=False, skip_group_check=True)
                        for k2 in range(kt + 1, 3):
                            n2 = P if k2 < 2 else LS
                            nc.tensor.matmul(o, C(C_NEG1, n, 0, n2), S[0:n2, 256 * k2:256 * (k2 + 1)],
                                             start=False, stop=False, skip_group_check=True)
                    for hh in range(SB_H):
                        at_ = B + 512 + LS * hh
                        last = nc.tensor.matmul(psf[0:LS, at_:at_ + LS], C(C_ID, LS, 0, LS),
                                                C(C_MASKNEG, LS, 0, LS), start=False, stop=True,
                                                skip_group_check=True)
                last.then_inc(cum_done, 1)

            def stick_out(h):
                W = se[:, h % 3, :]
                pe.wait_ge(sb_w, h + 1)
                if h < SB_H:
                    c, b = h // 2, 64 * (h % 2)
                    if h >= 4:
                        pe.wait_ge(so_mix, h // 2 - 1)
                    for j in range(TILES):
                        last = nc.tensor.matmul(bank(6 + c % 2, j * P, 512, b, b + 64),
                                                sv_n[:, j, h * 64:(h + 1) * 64], W[:, OFF[j]:OFF[j] + LEN[j]],
                                                start=(j == 0), stop=(j == TILES - 1))
                    last.then_inc(so_done, 1)
                else:
                    pe.wait_ge(so_mix, 3)
                    for hh in range(SB_H):
                        c, b = hh // 2, 64 * (hh % 2)
                        for kt in range(3):
                            n = P if kt < 2 else LS
                            v = vc_n[:, kt, hh * 64:(hh + 1) * 64] if kt < 2 else sv_n[0:LS, 4, hh * 64:(hh + 1) * 64]
                            at_ = 256 * kt + LS * hh
                            last = nc.tensor.matmul(bank(6, c * LS, (c + 1) * LS, b, b + 64), v,
                                                    W[0:n, at_:at_ + LS], start=(kt == 0), stop=(kt == 2),
                                                    skip_group_check=True)
                    last.then_inc(so_done, 1)

            pe.wait_ge(cr_ready, 4)
            pe.wait_ge(st_ready, 2)
            pe.wait_ge(ro_root, 4)
            stick_z(0)
            for h in range(SB_H + 1):
                if h + 1 <= SB_H:
                    stick_z(h + 1)
                stick_cum(h)
                if h:
                    stick_out(h - 1)
            stick_out(SB_H)
            pe.wait_ge(so_mix, 5)
            pe.wait_ge(ret_mix, 4)
            run(AB_OUT, a, None, 0)
            ffn(1, 2)

            ffn(2, 3)
            first_pair(CD_IN, 4)
            cc_ = STAGE[CD_IN][1:3]
            for i in range(2):
                if i:
                    run(CD_IN, u, None, 0, 1, 2)
                for s in range(2):
                    turn_chunk(tg[:, s, :], 8 + 2 * i + s, evac[s], cc_[s] + i + 1)
            run(CD_IN, u, None, 0, 2, 5, body=lambda i: [
                turn_chunk(tg[:, s, :], 12 + 2 * i + s, conv_src, 2 * i + s + 1) for s in range(2)])
            run(CD_IN, u, None, 0, 5, 12)
            _, c0, c1, count, K, _ = STAGE[CD_DT]
            product(0, c0, K, u, None, 0)
            pe.wait_ge(dt_ready, 1)
            pe.wait_ge(tp_free, 18)
            for t in range(5):
                n = P if t < TILES else LS
                last = nc.tensor.transpose(bank(6, 40 * t, 40 * t + 40, 0, n), dtda[0:40, t * P:t * P + n],
                                           C(C_ID, 40, 0, 40))
            last.then_inc(dtn_done, 1)
            pe.wait_ge(evac[0], c0 + 1)
            pe.wait_ge(evac[1], c1)

            pe.wait_ge(dtn_ready, 1)
            for t in range(5):
                n = P if t < TILES else LS
                r = slice(t * P, t * P + n)
                da = dtn[0:n, t, 32:40]
                if t:
                    pe.wait_ge(m_ready, t)
                nc.tensor.matmul(bank(0, 0, 8, 0, n), C(C_LE, n, 0, n), da, start=True, stop=True,
                                 skip_group_check=True)
                nc.tensor.matmul(bank(0, 8, 16, 0, n), C(C_GT, n, 0, n), da, start=True, stop=True,
                                 skip_group_check=True)
                nc.tensor.matmul(bank(0, 16, 24), C(C_ONE, P, 0, n), da, start=True, stop=True,
                                 skip_group_check=True).then_inc(g_done, 1)
                for g in range(SSD_G):
                    last = nc.tensor.matmul(bank(1, g * P, g * P + n, 0, n), bc_t[:, g, r], bc_t[:, 2 + g, r],
                                            start=True, stop=True, skip_group_check=True)
                last.then_inc(cb_done, 1)
                pe.wait_ge(hl_ready, t + 1)
                for h in range(SSD_H):
                    last = nc.tensor.matmul(bank(2 + h // 4, (h % 4) * P, (h % 4) * P + n, 0, n),
                                            hl[0:n, h, 0:n], C(C_LE, n, 0, n), start=True, stop=True,
                                            skip_group_check=True)
                last.then_inc(seg_done, 1)
                if t in (0, TILES):
                    pe.wait_ge(sst_loaded, 17)
                pe.wait_ge(sst_ready, 2 * t if t else 0)
                S = sst[:, 0 if t < TILES else 1, :]
                for g in range(SSD_G):
                    nc.tensor.matmul(bank(4, g * 256, (g + 1) * 256, 0, n), bc_t[:, 2 + g, r],
                                     S[:, g * 256:(g + 1) * 256], start=True, stop=True, skip_group_check=True)
                pe.wait_ge(m_ready, t + 1)
                pe.wait_ge(xw_ready, t + 1)
                for h in range(SSD_H):
                    last = nc.tensor.matmul(bank(5, h * 64, (h + 1) * 64, 0, n), seg[0:n, h, 0:n],
                                            xd[0:n, h * 64:(h + 1) * 64], start=True, stop=True,
                                            skip_group_check=True)
                last.then_inc(y_done, 1)
                if t == 0:
                    pe.wait_ge(dtn_ready, 1)
                for g in range(SSD_G):
                    last = nc.tensor.matmul(bank(6, g * 256, (g + 1) * 256), b_n[0:n, t, g * P:(g + 1) * P],
                                            xw[0:n, g * 256:(g + 1) * 256], start=True, stop=True,
                                            skip_group_check=True)
                last.then_inc(s_scaled, 1)
                pe.wait_ge(y_sum, t + 1)
                if t:
                    pe.wait_ge(yz_done, t)
                for c in range(4):
                    last = nc.tensor.transpose(bank(7, c * P, c * P + n), yn[0:n, c * P:(c + 1) * P],
                                               C(C_ID, n, 0, n))
                last.then_inc(yt_done, 1)
            pe.wait_ge(y_sq, 4)
            for c in range(4):
                for half in range(2):
                    last = nc.tensor.matmul(bank(half, 0, HT), C(C_ONE), yq[:, c, half * HT:(half + 1) * HT],
                                            start=(c == 0), stop=(c == 3))
            last.then_inc(yss_done, 1)

            items = [(h, t) for h in range(SB_H) for t in range(5)]

            def band_s(n):
                h, t = items[n]
                c, b = h // 2, 64 * (h % 2)
                B = 1 + n % 3
                if n >= 3:
                    pe.wait_ge(b_max, n - 2)
                if t < TILES:
                    w = (t + 1) * P
                    last = nc.tensor.matmul(bank(B, 0, w), bq_t[b:b + 64, c, t * P:(t + 1) * P],
                                            bk_t[b:b + 64, c, 0:w], start=True, stop=True)
                else:
                    nc.tensor.matmul(bank(B, 0, PAST, 0, LS), bqz[:, c, h % 2, :], kb_t[:, c, :],
                                     start=True, stop=True)
                    last = nc.tensor.matmul(bank(B, PAST, PAST + LS, 0, LS), bqz[:, c, h % 2, :],
                                            bk_t[:, c, LP:T], start=True, stop=True)
                last.then_inc(bs_done, 1)

            def band_turn(n):
                h, t = items[n]
                pe.wait_ge(b_exp, n + 1)
                if n >= 2:
                    pe.wait_ge(bp_copied, n - 1)
                p_ = pr[:, n % 3, :]
                if t < TILES:
                    for j in range(t + 1):
                        last = nc.tensor.transpose(bank(4 + n % 2, j * P, (j + 1) * P), p_[:, j * P:(j + 1) * P],
                                                   C(C_ID))
                else:
                    for j in range(3):
                        m = P if j < 2 else LS
                        last = nc.tensor.transpose(bank(4 + n % 2, j * LS, (j + 1) * LS, 0, m),
                                                   p_[0:LS, j * P:j * P + m], C(C_ID, LS, 0, LS))
                last.then_inc(bp_done, 1)

            def band_out(n):
                h, t = items[n]
                pe.wait_ge(bp_copied, n + 1)
                if n >= 2:
                    pe.wait_ge(bo_evac, n - 1)
                pt_ = pt[:, n % 2, :]
                if t < TILES:
                    for j in range(t + 1):
                        last = nc.tensor.matmul(bank(6 + n % 2, 0, 64), pt_[:, j * P:(j + 1) * P],
                                                bv_n[:, j, h * 64:(h + 1) * 64], start=(j == 0), stop=(j == t))
                else:
                    for j in range(3):
                        m = P if j < 2 else LS
                        v = vb_n[:, j, h * 64:(h + 1) * 64] if j < 2 else bv_n[0:LS, 4, h * 64:(h + 1) * 64]
                        last = nc.tensor.matmul(bank(6 + n % 2, 0, 64, 0, LS), pt_[0:m, j * LS:(j + 1) * LS], v,
                                                start=(j == 0), stop=(j == 2))
                last.then_inc(bo_done, 1)

            def band_back(c):
                pe.wait_ge(bo_evac, 10 * c + 10)
                if c:
                    pe.wait_ge(band_mix, 2 * c)
                for t in range(TILES):
                    last = nc.tensor.transpose(bank(0, t * P, (t + 1) * P), on[:, t, c * P:(c + 1) * P], C(C_ID))
                last.then_inc(bb_done, 1)
                pe.wait_ge(band_mix, 2 * c + 1)
                nc.tensor.transpose(bank(0, 0, LS), on[0:LS, 4, c * P:(c + 1) * P],
                                    C(C_ID, LS, 0, LS)).then_inc(bb_done, 1)

            pe.wait_ge(y_root, 1)
            pe.wait_ge(yz_done, 5)
            pe.wait_ge(bt_masked, 1)
            pe.wait_ge(cdc_loaded, 48)
            for n in range(len(items) + 3):
                if n < len(items):
                    band_s(n)
                if 2 <= n < len(items) + 2:
                    band_turn(n - 2)
                if n >= 3:
                    band_out(n - 3)
                if n >= 14 and (n - 14) % 10 == 0:
                    band_back((n - 14) // 10)
            band_back(3)
            pe.wait_ge(band_mix, 8)
            pe.wait_ge(ssd_mix, 4)
            run(CD_OUT, a, None, 0)
            ffn(3, 5)
            sum_squares(6)



        @block.scalar
        def _(act):
            steps = [0]

            def link(ins_):
                steps[0] += 1
                ins_.then_inc(act_step, 1)
                act.wait_ge(act_step, steps[0])

            act.dma_start(par[:], ins["par"]).then_inc(par_loaded, 16)
            for m in range(DC):
                act.dma_start(x[:, m, :], ins["x"][m]).then_inc(x_loaded[m], 16)
            act.dma_start(const[:], ins["const"]).then_inc(const_loaded, 16)
            act.dma_start(tab[:], ins["tab"]).then_inc(tab_loaded, 16)

            def square(n, m, wait_x):
                wait_x()
                if n or m >= 2:
                    act.wait_ge(ss_added, (DC - 1) * n + (max(m - 2, 1) if m >= 2 else 0))
                nc.scalar.activation(sq[:, m % 2, :], x[:, m, :], ACT.Square).then_inc(sq_done, 1)

            def root(n):
                act.wait_ge(ss_total, n + 1)
                if n:
                    act.wait_ge(rstd_ready, n)
                nc.scalar.activation(halves(rms[:]), pair(4), ACT.Sqrt, bias=par[:, P_EPS:P_EPS + 1],
                                     scale=1.0 / D).then_inc(rms_root, 1)

            def squares_after(stage, n):
                _, c0, c1, _, _, _ = STAGE[stage]
                for m in range(DC):
                    square(n, m, lambda: act.wait_ge(evac[m % 2], (c0, c1)[m % 2] + m // 2 + 1))

            def ffn(f, n):
                root(n)
                for g in range(G):
                    _, c0, _, _, _, _ = STAGE[FFN_STAGE[f] + 2 * g]
                    with act.Fori(0, GC) as i:
                        act.wait_ge(evac[0], c0 + i + 1)
                        nc.scalar.activation(sil[:], tg[:, 0, :], ACT.Silu).then_inc(sil_done, 1)
                squares_after(FFN_STAGE[f] + 3, n + 1)

            turned = [0]

            def take_turned(dst, lo):
                act.wait_ge(tp_done, turned[0] + 1)
                nc.scalar.copy(dst[:, 0:TILES, lo:lo + P], bank(6).rearrange("p (t c) -> p t c", t=TILES))
                nc.scalar.copy(dst[0:LS, 4, lo:lo + P], bank(7, 0, P, 0, LS)).then_inc(tp_free, 1)
                turned[0] += 1

            for m in range(DC):
                square(0, m, lambda: act.wait_ge(x_loaded[m], 16))
            act.wait_ge(par_loaded, 16)
            ffn(0, 0)
            root(1)
            act.dma_start(s0[:], ins["s_ret"]).then_inc(cache_loaded, 16)
            for c in range(4):
                take_turned(rv_n, c * P)
            for c in range(4):
                act.wait_ge(evac[c % 2], STAGE[AB_IN][1 + c % 2] + 2 + c // 2 + 1)
                act.dma_start(outs["sv"][c], tg[:, c % 2, :]).then_inc(skv_out[c % 2], 16)
                take_turned(sv_n, c * P)
            _, c0, c1, _, _, _ = STAGE[AB_IN]
            for c in range(4):
                p_, s = 6 + c // 2, c % 2
                act.wait_ge(evac[s], (c0, c1)[s] + p_ + 1)
                nc.scalar.activation(rg[:, c, :], tg[:, s, :], ACT.Silu).then_inc(rg_ready, 1)
            for c in range(4):
                p_, s = 10 + c // 2, c % 2
                act.wait_ge(evac[s], (c0, c1)[s] + p_ + 1)
                act.dma_start(outs["sk"][c], sk_t[:, c, :]).then_inc(out_done, 16)
            for h in range(RET_H):
                act.wait_ge(ro_evac, 2 * h + 2)
                nc.scalar.activation(rsq[:, h, :], ro[:, h, :], ACT.Square).then_inc(ro_sq, 1)
            for h in range(RET_H):
                act.wait_ge(ro_ss, h + 1)
                nc.scalar.activation(halves(rsq[:, h, :]), pair(2 * h), ACT.Sqrt,
                                     bias=par[:, P_EPS:P_EPS + 1], scale=1.0 / RET_DV).then_inc(ro_root, 1)
            act.wait_ge(st_ready, 2)
            act.dma_start(outs["p_ret"], sil[:, 0:256].rearrange("p (c e) -> p c e", c=2)).then_inc(out_done, 16)
            act.dma_start(outs["s_ret"], sil[:, 256:512].rearrange("p (c e) -> p c e", c=2)).then_inc(out_done, 16)

            act.dma_start(kc_t[:], ins["kc"]).then_inc(cache_loaded, 16)
            act.dma_start(vc_n[:], ins["vc"]).then_inc(cache_loaded, 16)

            def stick_parts(h):
                return [(slice(0, P), slice(0, ZW))] if h < SB_H else [
                    (slice(0, P), slice(0, 512)), (slice(0, LS), slice(512, 768))]

            def stick_ln(h):
                act.wait_ge(z_done, h + 1)
                if h >= 3:
                    act.wait_ge(so_done, h - 2)
                B = 512 * 3 * (h % 2)
                for r, cc in stick_parts(h):
                    last = nc.scalar.activation(se[r, h % 3, cc], psf[r, B + cc.start:B + cc.stop], ACT.Abs)
                link(last)
                for r, cc in stick_parts(h):
                    e = se[r, h % 3, cc]
                    last = nc.scalar.activation(e, e, ACT.Exp, scale=-1.0)
                link(last)
                for r, cc in stick_parts(h):
                    e = se[r, h % 3, cc]
                    last = nc.scalar.activation(e, e, ACT.Ln, bias=par[r, P_EPS + 1:P_EPS + 2])
                last.then_inc(sb_ln, 1)

            def stick_w(h):
                act.wait_ge(cum_done, h + 1)
                act.wait_ge(sb_sp, h + 1)
                B = 512 * 3 * (h % 2)
                for r, cc in stick_parts(h):
                    last = nc.scalar.activation(se[r, h % 3, cc], psf[r, B + cc.start:B + cc.stop], ACT.Exp)
                last.then_inc(sb_w, 1)

            stick_ln(0)
            for h in range(SB_H + 1):
                if h + 1 <= SB_H:
                    stick_ln(h + 1)
                stick_w(h)
            squares_after(AB_OUT, 2)
            ffn(1, 2)
            act.dma_start(bt[:], ins["bias"]).then_inc(bt_loaded, 16)
            ffn(2, 3)
            root(4)
            act.dma_start(cs[:], ins["conv"]).then_inc(cdc_loaded, 16)
            for c in range(4):
                act.wait_ge(evac[c % 2], STAGE[CD_IN][1 + c % 2] + c // 2 + 1)
                act.dma_start(outs["bv"][c], tg[:, c % 2, :]).then_inc(skv_out[c % 2], 16)
                take_turned(bv_n, c * P)
            for c in range(8):
                s = c % 2
                act.wait_ge(conv_acc, c + 1)
                if c < 6:
                    act.wait_ge(tp_done, 12 + c - 1 if c >= 2 else 12)
                    dst = tg[:, s, :]
                    nc.scalar.activation(dst[:, 0:LP], cacc[:, 0:LP], ACT.Silu)
                    nc.scalar.activation(dst[:, LP:T], cacc[:, LP + 3:LP + 3 + LS], ACT.Silu).then_inc(conv_src, 1)
                    take_turned(xs_n if c < 4 else b_n, (c % 4) * P)
                    if c >= 4:
                        nc.scalar.copy(bc_t[:, c - 4, :], dst).then_inc(conv_out, 1)
                else:
                    dst = bc_t[:, c - 4, :]
                    nc.scalar.activation(dst[:, 0:LP], cacc[:, 0:LP], ACT.Silu)
                    nc.scalar.activation(dst[:, LP:T], cacc[:, LP + 3:LP + 3 + LS], ACT.Silu).then_inc(conv_out, 1)
            _, c0, c1, _, _, _ = STAGE[CD_IN]
            for c in range(4):
                p_, s = 6 + c // 2, c % 2
                act.wait_ge(evac[s], (c0, c1)[s] + p_ + 1)
                nc.scalar.activation(zs[:, c, :], tg[:, s, :], ACT.Silu).then_inc(z_silu, 1)
            for c in range(4):
                p_, s = 10 + c // 2, c % 2
                act.wait_ge(evac[s], (c0, c1)[s] + p_ + 1)
                act.dma_start(outs["bk"][c], bk_t[:, c, :]).then_inc(out_done, 16)
            act.wait_ge(prod_done[0], STAGE[CD_DT][1] + 1)
            act.dma_start(sst[:, 1, :], ins["s_ssm"]).then_inc(sst_loaded, 16)
            act.wait_ge(cdc_loaded, 16)
            nc.scalar.activation(ea[0:8, :], par[0:8, P_ALOG:P_ALOG + 1], ACT.Exp).then_inc(a_neg, 1)
            act.wait_ge(dt_evac, 1)
            link(nc.scalar.activation(dtl[0:8, :], tg[0:8, 0, :], ACT.Abs))
            link(nc.scalar.activation(dtl[0:8, :], dtl[0:8, :], ACT.Exp, scale=-1.0))
            nc.scalar.activation(dtl[0:8, :], dtl[0:8, :], ACT.Ln, bias=par[0:8, P_EPS + 1:P_EPS + 2]).then_inc(dt_ln, 1)
            for t in range(5):
                n = P if t < TILES else LS
                act.wait_ge(g_done, t + 1)
                if t:
                    act.wait_ge(sst_ready, 2 * t)
                nc.scalar.activation(eg[0:n, 0:16], bank(0, 0, 16, 0, n), ACT.Exp)
                nc.scalar.activation(eg[:, 16:24], bank(0, 16, 24), ACT.Exp).then_inc(g_exp, 1)
                act.wait_ge(seg_done, t + 1)
                if t:
                    act.wait_ge(y_done, t)
                nc.scalar.activation(seg[0:n, :, 0:n], ps[0:n, 2:4, :].rearrange(
                    "p a (h c) -> p (a h) c", h=4)[:, :, 0:n], ACT.Exp).then_inc(seg_exp, 1)
            for c in range(4):
                act.wait_ge(yz_done, 5)
                nc.scalar.activation(yq[:, c, :], yz[:, c, :], ACT.Square).then_inc(y_sq, 1)
            act.wait_ge(yss_done, 1)
            act.wait_ge(rstd_ready, 5)
            nc.scalar.activation(halves(rms[:]), pair(0), ACT.Sqrt, bias=par[:, P_EPS:P_EPS + 1],
                                 scale=1.0 / (SSD_H * SSD_P)).then_inc(y_root, 1)
            act.wait_ge(sst_ready, 10)
            act.dma_start(outs["ssm"], sst[:]).then_inc(out_done, 16)
            act.dma_start(outs["conv"], cnew[:]).then_inc(conv_left, 16)
            act.dma_start(kb_t[:], ins["kb"]).then_inc(cdc_loaded, 16)
            act.dma_start(vb_n[:], ins["vb"]).then_inc(cdc_loaded, 16)
            items = [(h, t) for h in range(SB_H) for t in range(5)]

            def band_width(n):
                h, t = items[n]
                return (P, (t + 1) * P) if t < TILES else (LS, PAST + LS)

            def band_exp(n):
                r, w = band_width(n)
                act.wait_ge(b_max, n + 1)
                p_, b = pr[0:r, n % 3, 0:w], bst[0:r, n % 3, :]
                nc.scalar.activation(p_, p_, ACT.Exp, bias=b[:, 1:2], accum_out=b[:, 2:3]).then_inc(b_exp, 1)

            def band_copy(n):
                h, t = items[n]
                act.wait_ge(bp_done, n + 1)
                if n >= 2:
                    act.wait_ge(bo_done, n - 1)
                if t < TILES:
                    w = (t + 1) * P
                    nc.scalar.copy(pt[:, n % 2, 0:w], bank(4 + n % 2, 0, w)).then_inc(bp_copied, 1)
                else:
                    nc.scalar.copy(pt[:, n % 2, 0:64], bank(4 + n % 2, 0, 64))
                    nc.scalar.copy(pt[0:LS, n % 2, 64:96], bank(4 + n % 2, 64, 96, 0, LS)).then_inc(bp_copied, 1)

            for n in range(len(items) + 2):
                if n < len(items):
                    band_exp(n)
                if n >= 2:
                    band_copy(n - 2)
            squares_after(CD_OUT, 5)
            ffn(3, 5)
            root(6)
            for m in range(DC):
                act.wait_ge(y_ready, m + 1)
                act.dma_start(outs["y"][m], yout[:, m, :]).then_inc(out_done, 16)
            for s in range(2):
                act.wait_ge(skv_out[s], 16 * 4)
            act.wait_ge(conv_left, 16)
            act.wait_ge(out_done, 16 * (4 + 2 + 4 + 1 + 8))


        @block.vector
        def _(dve):
            V = nc.vector
            steps = [0]

            def link(ins_):
                steps[0] += 1
                ins_.then_inc(dve_step, 1)
                dve.wait_ge(dve_step, steps[0])

            def split(dst_hi, dst_lo, src, hi_sem, hi_count, out_sem):
                V.tensor_scalar(dst_hi, src, 1.0, None, ALU.mult).then_inc(hi_sem, 1)
                dve.wait_ge(hi_sem, hi_count)
                V.tensor_tensor(dst_lo, src, dst_hi.bitcast(F32), ALU.subtract).then_inc(out_sem, 1)

            def norm_chunk(n, m):
                g = par[:, P_NORM + 8 * n + m:P_NORM + 8 * n + m + 1]
                V.tensor_scalar(u[:, m, 0, :], x[:, m, :], g, None, ALU.mult).then_inc(u_high, 1)
                dve.wait_ge(u_high, DC * n + m + 1)
                V.scalar_tensor_tensor(u[:, m, 1, :], x[:, m, :], g, u[:, m, 0, :].bitcast(F32), ALU.mult,
                                       ALU.subtract).then_inc(u_ready, 1)

            def add_squares(n, m):
                dve.wait_ge(sq_done, DC * n + m + 1)
                if m == 1:
                    if n:
                        dve.wait_ge(ss_total, n)
                    V.tensor_tensor(ssum[:], sq[:, 0, :], sq[:, 1, :], ALU.add).then_inc(ss_added, 1)
                elif m:
                    dve.wait_ge(ss_added, (DC - 1) * n + m - 1)
                    V.tensor_tensor(ssum[:], ssum[:], sq[:, m % 2, :], ALU.add).then_inc(ss_added, 1)

            def inv_rms(n):
                dve.wait_ge(rms_root, n + 1)
                V.reciprocal(rstd[:], rms[:]).then_inc(rstd_ready, 1)
                dve.wait_ge(rstd_ready, n + 1)

            def residual(stage, factor, n=None):
                _, c0, c1, _, _, _ = STAGE[stage]
                for m in range(DC):
                    s, c = m % 2, (c0, c1)[m % 2] + m // 2 + 1
                    dve.wait_ge(prod_done[s], c)
                    V.scalar_tensor_tensor(halves(x[:, m, :]), pair(2 * s), factor, halves(x[:, m, :]), ALU.mult,
                                           ALU.add).then_inc(evac[s], 1)
                    if n is not None:
                        dve.wait_ge(evac[s], c)
                        if n < NORMS - 1:
                            norm_chunk(n, m)
                        if m:
                            add_squares(n, m - 1)
                if n is not None:
                    add_squares(n, DC - 1)

            def scaled(s, count, dst, factor=None, rows=P):
                dve.wait_ge(prod_done[s], count)
                src = ps[0:rows, 2 * s:2 * s + 2, 0:HT]
                if factor is None:
                    V.tensor_tensor(halves(dst), src, halves(rstd[0:rows, :]), ALU.mult).then_inc(evac[s], 1)
                else:
                    V.scalar_tensor_tensor(halves(dst), src, factor, halves(rstd[0:rows, :]), ALU.mult,
                                           ALU.mult).then_inc(evac[s], 1)

            def ffn(f, n):
                inv_rms(n)
                for g in range(G):
                    st = FFN_STAGE[f] + 2 * g
                    _, c0, c1, _, _, _ = STAGE[st]
                    done = FC * f + GC * g
                    with dve.Fori(0, GC) as i:
                        scaled(0, c0 + i + 1, tg[:, 0, :])
                        scaled(1, c1 + i + 1, tg[:, 1, :])
                        dve.wait_ge(evac[1], c1 + i + 1)
                        dve.wait_ge(sil_done, done + i + 1)
                        V.tensor_tensor(tg[:, 1, :], tg[:, 1, :], sil[:], ALU.mult).then_inc(glu_done, 1)
                        dve.wait_ge(glu_done, done + i + 1)
                        hi = a[:, bass.ds(i, 1), 0, :].rearrange("p a t -> p (a t)")
                        lo = a[:, bass.ds(i, 1), 1, :].rearrange("p a t -> p (a t)")
                        split(hi, lo, tg[:, 1, :], act_high, done + i + 1, act_ready)
                        dve.wait_ge(act_ready, done + i + 1)
                    residual(st + 1, 0.5, n + 1 if g == 1 else None)

            dve.wait_ge(par_loaded, 16)
            for m in range(DC):
                dve.wait_ge(x_loaded[m], 16)
                norm_chunk(0, m)
            for m in range(DC):
                add_squares(0, m)
            dve.wait_ge(const_loaded, 16)
            ffn(0, 0)

            _, c0, c1, _, _, _ = STAGE[AB_IN]

            def count(p_, s):
                return (c0, c1)[s] + p_ + 1

            def values(p0, chunks, turned0, leave0):
                for c in range(chunks):
                    s = c % 2
                    if turned0 + c >= 2:
                        dve.wait_ge(tp_done, turned0 + c - 1)
                    if leave0 is not None and leave0 + c // 2 > 0:
                        dve.wait_ge(skv_out[s], 16 * (leave0 + c // 2))
                    scaled(s, count(p0 + c // 2, s), tg[:, s, :])

            inv_rms(1)
            values(0, 4, 0, None)
            values(2, 4, 4, 0)
            for s in range(2):
                dve.wait_ge(skv_out[s], 16 * 2)
            dve.wait_ge(tp_done, 8)
            dve.wait_ge(tab_loaded, 16)
            for c in range(4):
                s = c % 2
                scaled(s, count(4 + c // 2, s), tg[:, s, :])
                dve.wait_ge(evac[s], count(4 + c // 2, s))
                V.tensor_tensor(rqk[:, c, :], tg[:, s, :], tab[:, A_COS:A_COS + T], ALU.mult).then_inc(rot_src, 1)
                dve.wait_ge(rot_done, c + 1)
                V.tensor_tensor(halves(tg[:, s, :]), pair(4), halves(tab[:, A_SIN:A_SIN + T]),
                                ALU.mult).then_inc(rot_free, 1)
                dve.wait_ge(rot_free, c + 1)
                dve.wait_ge(rot_src, c + 1)
                link(V.tensor_tensor(rqk[:, c, :], rqk[:, c, :], tg[:, s, :], ALU.add))
            for c in range(4):
                s = c % 2
                if c >= 2:
                    dve.wait_ge(rg_ready, c - 1)
                scaled(s, count(6 + c // 2, s), tg[:, s, :])
            for c in range(4):
                scaled(c % 2, count(8 + c // 2, c % 2), sq_t[:, c, :], DH ** -0.5)
            for c in range(4):
                scaled(c % 2, count(10 + c // 2, c % 2), sk_t[:, c, :])
            dve.wait_ge(prod_done[1], count(11, 1))
            for to, at_ in ((CR_NEGT, C_NEGT), (CR_NEG1, C_NEG1), (CR_ID, C_ID), (CR_MASK, C_MASKNEG)):
                V.tensor_scalar(cr[:, to, :], C(at_), 1.0, None, ALU.mult).then_inc(cr_ready, 1)
            V.memset(qs[:], 0.0)
            link(V.memset(sqz[:], 0.0))
            for i in range(2):
                r = slice(64 * i, 64 * i + 64)
                V.tensor_tensor(qs[r, :, i, :], rqk[r, 0:2, LP:T],
                                const[r, C_QDEC:C_QDEC + 64].rearrange("p (c t) -> p c t", c=2), ALU.mult)
                last = V.tensor_copy(sqz[r, :, i, :], sq_t[r, :, LP:T])
            last.then_inc(qs_ready, 1)
            for c in range(2):
                dve.wait_ge(kt_done, c + 1)
                kdec = C(C_KDEC, 16).rearrange("p (t h) -> p t h", h=4)[:, :, 2 * c:2 * c + 2]
                V.tensor_tensor(kd[:, 0:TILES, c * P:(c + 1) * P].rearrange("p t (h d) -> p t h d", h=2),
                                bank(6).rearrange("p (t h d) -> p t h d", t=TILES, h=2),
                                kdec.unsqueeze(3).broadcast_to([P, TILES, 2, 64]), ALU.mult).then_inc(kd_ready, 1)
                ks = const[0:LS, C_KDEC + 16 + 2 * c:C_KDEC + 18 + 2 * c]
                V.tensor_tensor(kd[0:LS, 4, c * P:(c + 1) * P].rearrange("p (h d) -> p h d", h=2),
                                bank(7, 0, P, 0, LS).rearrange("p (h d) -> p h d", h=2),
                                ks.unsqueeze(2).broadcast_to([LS, 2, 64]), ALU.mult).then_inc(kd_ready, 1)

            def ret_att(h):
                dve.wait_ge(rs_done, h + 1)
                if h >= 2:
                    dve.wait_ge(ro_done, h - 1)
                B = 512 * 3 * (h % 2)
                for j in range(TILES):
                    V.tensor_tensor(att[:, h % 2, OFF[j]:OFF[j] + LEN[j]], psf[:, B + OFF[j]:B + OFF[j] + LEN[j]],
                                    tab[:, A_DEC + LP * h:A_DEC + LP * h + LEN[j]], ALU.mult)
                V.tensor_tensor(att[0:LS, h % 2, ZW:ZW + LS], psf[0:LS, B + ZW:B + ZW + LS],
                                tab[0:LS, A_DEC + LP * h:A_DEC + LP * h + LS], ALU.mult).then_inc(rs_att, 1)

            ret_att(0)
            for h in range(RET_H):
                if h + 1 < RET_H:
                    ret_att(h + 1)
                dve.wait_ge(ro_done, h + 1)
                V.tensor_copy(ro[:, h, 0:LP], bank(6)).then_inc(ro_evac, 1)
                V.tensor_copy(ro[:, h, LP:T], bank(7, 0, LS)).then_inc(ro_evac, 1)

            def ret_norm(h):
                dve.wait_ge(ro_root, h + 1)
                dve.wait_ge(rg_ready, h + 1)
                link(V.reciprocal(rsq[:, h, :], rsq[:, h, :]))
                link(V.tensor_tensor(ro[:, h, :], ro[:, h, :], rsq[:, h, :], ALU.mult))
                link(V.scalar_tensor_tensor(rg[:, h, :], ro[:, h, :], par[:, P_RET + h:P_RET + h + 1], rg[:, h, :],
                                            ALU.mult, ALU.mult))

            def ret_split(h):
                link(V.tensor_scalar(a[:, h, 0, :], rg[:, h, :], 1.0, None, ALU.mult))
                V.tensor_tensor(a[:, h, 1, :], rg[:, h, :], a[:, h, 0, :].bitcast(F32),
                                ALU.subtract).then_inc(ret_mix, 1)

            dve.wait_ge(st_done, 1)
            dve.wait_ge(cache_loaded, 16)
            V.tensor_copy(sil[:, 0:256], bank(0, 0, 256)).then_inc(st_ready, 1)
            for h in range(RET_H):
                c, b = h // 2, 64 * (h % 2)
                last = V.scalar_tensor_tensor(sil[b:b + 64, 256 + c * P:256 + (c + 1) * P], s0[b:b + 64, c, :],
                                              float(ret_cdec[h]), bank(1, c * P, (c + 1) * P, b, b + 64),
                                              ALU.mult, ALU.add)
            last.then_inc(st_ready, 1)

            strict = C(C_STRICT)

            def stick_parts(h):
                return [(slice(0, P), slice(0, ZW))] if h < SB_H else [
                    (slice(0, P), slice(0, 512)), (slice(0, LS), slice(512, 768))]

            def stick_sp(h):
                dve.wait_ge(sb_ln, h + 1)
                B = 512 * 3 * (h % 2)
                S = se[:, h % 3, :]
                for r, cc in stick_parts(h):
                    last = V.scalar_tensor_tensor(S[r, cc], psf[r, B + cc.start:B + cc.stop], 0.0, S[r, cc],
                                                  ALU.max, ALU.add)
                link(last)
                if h == SB_H:
                    d = S[0:LS, 512:768].rearrange("p (h q) -> p h q", h=SB_H)
                    V.tensor_tensor(d, d, C(C_STRICT, LS, 0, LS).unsqueeze(1).broadcast_to([LS, SB_H, LS]),
                                    ALU.mult).then_inc(sb_sp, 1)
                    return
                d = S[:, 0:1280].rearrange("p (a b) -> p a b", b=P)[:, 0:9:4, :]
                V.tensor_tensor(d, d, strict.unsqueeze(1).broadcast_to([P, 3, P]), ALU.mult)
                d = S[:, OFF[3]:OFF[3] + P]
                link(V.tensor_tensor(d, d, strict, ALU.mult))
                if h >= 2:
                    dve.wait_ge(cum_done, h - 1)
                V.tensor_scalar(sps[h % 2][:, 0, :], S, 1.0, None, ALU.mult).then_inc(sb_high, 1)
                dve.wait_ge(sb_high, h + 1)
                V.tensor_tensor(sps[h % 2][:, 1, :], S, sps[h % 2][:, 0, :].bitcast(F32),
                                ALU.subtract).then_inc(sb_sp, 1)

            def stick_mix(c):
                dve.wait_ge(so_done, 2 * c + 2)
                src = bank(6 + c % 2)
                link(V.tensor_scalar(a[:, 4 + c, 0, 0:LP], src, 1.0, None, ALU.mult))
                V.tensor_tensor(a[:, 4 + c, 1, 0:LP], src, a[:, 4 + c, 0, 0:LP].bitcast(F32),
                                ALU.subtract).then_inc(so_mix, 1)

            for h in range(SB_H + 1):
                stick_sp(h)
                if h < 4:
                    ret_norm(h)
                elif h < 6:
                    ret_split(2 * h - 8)
                    ret_split(2 * h - 7)
                if h >= 3 and h % 2 == 1:
                    stick_mix((h - 3) // 2)
            stick_mix(3)
            dve.wait_ge(so_done, SB_H + 1)
            src = bank(6, 0, P).rearrange("p (c q) -> p c q", c=4)
            link(V.tensor_scalar(a[:, 4:8, 0, LP:T], src, 1.0, None, ALU.mult))
            V.tensor_tensor(a[:, 4:8, 1, LP:T], src, a[:, 4:8, 0, LP:T].bitcast(F32),
                            ALU.subtract).then_inc(so_mix, 1)
            residual(AB_OUT, 1.0, 2)
            ffn(1, 2)
            dve.wait_ge(bt_loaded, 16)
            V.memset(bt[0:64, :, 448:512], NEG).then_inc(bt_masked, 1)
            ffn(2, 3)

            _, c0, c1, _, _, _ = STAGE[CD_IN]
            inv_rms(4)
            values(0, 4, 8, 2)
            for s in range(2):
                dve.wait_ge(skv_out[s], 16 * 4)
            dve.wait_ge(tp_done, 12)
            dve.wait_ge(cdc_loaded, 16)
            V.memset(xpad[:, :, 0:3], 0.0)
            link(V.memset(dtda[:], 0.0))
            for c in range(8):
                s = c % 2
                p_ = 2 + c // 2
                X = xpad[:, s, :]
                dve.wait_ge(prod_done[s], count(p_, s))
                V.tensor_copy(X[:, 515:518], cs[:, c, :])
                V.tensor_tensor(X[:, 3:3 + HT], bank(2 * s, 0, HT), rstd[:, 0:HT], ALU.mult)
                V.tensor_tensor(X[:, 3 + HT:3 + LP], bank(2 * s + 1, 0, LP - HT), rstd[:, HT:LP], ALU.mult)
                V.tensor_tensor(X[:, 518:550], bank(2 * s + 1, LP - HT, HT), rstd[:, LP:T],
                                ALU.mult).then_inc(evac[s], 1)
                dve.wait_ge(evac[s], count(p_, s))
                V.tensor_copy(cnew[:, c, 0, :], X[:, LP:LP + 3])
                V.tensor_copy(cnew[:, c, 1, :], X[:, 547:550])
                w = [par[:, P_CW + 8 * i + c:P_CW + 8 * i + c + 1] for i in range(TAPS)]
                if c >= 1:
                    if c <= 6:
                        dve.wait_ge(conv_src, c)
                    else:
                        dve.wait_ge(conv_out, c - 4)
                link(V.tensor_scalar(cacc[:], X[:, 0:547], w[0], par[:, P_CB + c:P_CB + c + 1], ALU.mult, ALU.add))
                for i in range(1, TAPS):
                    last = V.scalar_tensor_tensor(cacc[:], X[:, i:i + 547], w[i], cacc[:], ALU.mult, ALU.add)
                    if i < TAPS - 1:
                        link(last)
                last.then_inc(conv_acc, 1)
            dve.wait_ge(tp_done, 18)
            dve.wait_ge(conv_out, 4)
            for c in range(4):
                s = c % 2
                if c >= 2:
                    dve.wait_ge(z_silu, c - 1)
                scaled(s, count(6 + c // 2, s), tg[:, s, :])
            for c in range(4):
                scaled(c % 2, count(8 + c // 2, c % 2), bq_t[:, c, :], DH ** -0.5)
            for c in range(4):
                scaled(c % 2, count(10 + c // 2, c % 2), bk_t[:, c, :])
            dve.wait_ge(z_silu, 4)
            cdt = STAGE[CD_DT][1] + 1
            scaled(0, cdt, tg[0:8, 0, :], rows=8)
            dve.wait_ge(evac[0], cdt)
            V.tensor_scalar(tg[0:8, 0, :], tg[0:8, 0, :], par[0:8, P_DTB:P_DTB + 1], None, ALU.add).then_inc(dt_evac, 1)
            dve.wait_ge(dt_ln, 1)
            link(V.scalar_tensor_tensor(dtda[0:8, :], tg[0:8, 0, :], 0.0, dtl[0:8, :], ALU.max, ALU.add))
            dve.wait_ge(a_neg, 1)
            V.tensor_scalar(dtda[32:40, :], dtda[0:8, :], ea[0:8, :], -1.0, ALU.mult, ALU.mult).then_inc(dt_ready, 1)
            dve.wait_ge(dtn_done, 1)
            V.tensor_copy(dtn[:, 0:TILES, :], bank(6, 0, 160).rearrange("p (t c) -> p t c", t=TILES))
            V.tensor_copy(dtn[0:LS, 4, :], bank(6, 160, 200, 0, LS)).then_inc(dtn_ready, 1)
            link(V.memset(bqz[:], 0.0))
            for i in range(2):
                r = slice(64 * i, 64 * i + 64)
                V.tensor_copy(bqz[r, :, i, :], bq_t[r, :, LP:T])
            V.memset(sst[:, 0, :], 0.0).then_inc(sst_loaded, 1)
            dve.wait_ge(dtn_ready, 1)
            dve.wait_ge(sst_loaded, 17)

            def heads(ap, n, width=64):
                return ap.unsqueeze(2).broadcast_to([n, SSD_H, width])

            for t in range(5):
                n = P if t < TILES else LS
                S = sst[:, 0 if t < TILES else 1, :]
                if t:
                    dve.wait_ge(s_scaled, t)
                    dve.wait_ge(seg_done, t)
                V.tensor_tensor(hl[0:n, :, 0:n], C(C_GT, n, 0, n).unsqueeze(1).broadcast_to([n, SSD_H, n]),
                                heads(dtn[0:n, t, 32:40], n, n), ALU.mult).then_inc(hl_ready, 1)
                X3 = xs_n[0:n, t, :].rearrange("p (h d) -> p h d", h=SSD_H)
                v3 = lambda tt, n=n: tt[0:n, :].rearrange("p (h d) -> p h d", h=SSD_H)
                if t == 0:
                    dve.wait_ge(tp_free, 18)
                link(V.tensor_tensor(v3(xd), X3, heads(dtn[0:n, t, 0:8], n), ALU.mult))
                dve.wait_ge(g_exp, t + 1)
                V.tensor_tensor(v3(xw), v3(xd), heads(eg[0:n, 8:16], n), ALU.mult).then_inc(xw_ready, 1)
                dve.wait_ge(cb_done, t + 1)
                link(V.tensor_tensor(cbm[0:n, :, 0:n], bank(1, 0, 256, 0, n).rearrange(
                    "p (g c) -> p g c", g=2)[:, :, 0:n], C(C_LE, n, 0, n).unsqueeze(1).broadcast_to(
                    [n, SSD_G, n]), ALU.mult))
                dve.wait_ge(seg_exp, t + 1)
                for g in range(SSD_G):
                    sg = seg[0:n, 4 * g:4 * g + 4, 0:n]
                    last = V.tensor_tensor(sg, sg, cbm[0:n, g:g + 1, 0:n].broadcast_to([n, 4, n]), ALU.mult)
                last.then_inc(m_ready, 1)
                dsk = heads(par[0:n, P_DSKIP:P_DSKIP + 8], n)
                V.tensor_tensor(v3(yt), X3, dsk, ALU.mult)
                dve.wait_ge(y_done, t + 1)
                if t:
                    dve.wait_ge(yt_done, t)
                link(V.tensor_tensor(v3(yn), bank(4, 0, 512, 0, n).rearrange("p (h d) -> p h d", h=SSD_H),
                                     heads(eg[0:n, 0:8], n), ALU.mult))
                link(V.tensor_tensor(yn[0:n, :], yn[0:n, :], yt[0:n, :], ALU.add))
                V.tensor_tensor(yn[0:n, :], bank(5, 0, 512, 0, n), yn[0:n, :], ALU.add).then_inc(y_sum, 1)
                dve.wait_ge(s_scaled, t + 1)
                V.tensor_tensor(v3(S, n=P), v3(S, n=P), heads(eg[:, 16:24], P), ALU.mult).then_inc(sst_ready, 1)
                dve.wait_ge(sst_ready, 2 * t + 1)
                V.tensor_tensor(S, bank(6), S, ALU.add).then_inc(sst_ready, 1)
                dve.wait_ge(sst_ready, 2 * t + 2)
                dve.wait_ge(yt_done, t + 1)
                if t == 0:
                    dve.wait_ge(z_silu, 4)
                V.tensor_tensor(yz[:, :, t * P:t * P + n], bank(7).rearrange("p (c r) -> p c r", c=4)[:, :, 0:n],
                                zs[:, :, t * P:t * P + n], ALU.mult).then_inc(yz_done, 1)
            dve.wait_ge(y_root, 1)
            link(V.reciprocal(rstd[:], rms[:]))
            for c in range(4):
                link(V.scalar_tensor_tensor(yz[:, c, :], yz[:, c, :], par[:, P_SSD + c:P_SSD + c + 1], rstd[:],
                                            ALU.mult, ALU.mult))
                link(V.tensor_scalar(a[:, c, 0, :], yz[:, c, :], 1.0, None, ALU.mult))
                V.tensor_tensor(a[:, c, 1, :], yz[:, c, :], a[:, c, 0, :].bitcast(F32),
                                ALU.subtract).then_inc(ssd_mix, 1)

            items = [(h, t) for h in range(SB_H) for t in range(5)]

            def band_max(n):
                h, t = items[n]
                dve.wait_ge(bs_done, n + 1)
                if n >= 3:
                    dve.wait_ge(bp_done, n - 2)
                b = bst[0:P if t < TILES else LS, n % 3, :]
                if t < TILES:
                    w, bias = (t + 1) * P, bt[:, h, (3 - t) * P:512]
                else:
                    w, bias = PAST + LS, bt[0:LS, h, P:P + PAST + LS]
                r = P if t < TILES else LS
                link(V.tensor_tensor_reduce(pr[0:r, n % 3, 0:w], bank(1 + n % 3, 0, w, 0, r), bias, 1.0, -3e38,
                                            ALU.add, ALU.max, b[:, 0:1]))
                V.tensor_scalar(b[:, 1:2], b[:, 0:1], -1.0, None, ALU.mult).then_inc(b_max, 1)

            def band_rows(n):
                h, t = items[n]
                r = P if t < TILES else LS
                b = bst[0:r, n % 3, :]
                dve.wait_ge(bo_done, n + 1)
                link(V.reciprocal(b[:, 3:4], b[:, 2:3]))
                V.tensor_scalar(on[0:r, t, h * 64:(h + 1) * 64], bank(6 + n % 2, 0, 64, 0, r), b[:, 3:4], None,
                                ALU.mult).then_inc(bo_evac, 1)

            def band_mix_(c):
                for k, (src, q) in enumerate(((bank(0), slice(0, LP)), (bank(0, 0, LS), slice(LP, T)))):
                    dve.wait_ge(bb_done, 2 * c + k + 1)
                    link(V.tensor_scalar(a[:, 4 + c, 0, q], src, 1.0, None, ALU.mult))
                    V.tensor_tensor(a[:, 4 + c, 1, q], src, a[:, 4 + c, 0, q].bitcast(F32),
                                    ALU.subtract).then_inc(band_mix, 1)

            dve.wait_ge(ssd_mix, 4)
            for n in range(len(items) + 3):
                if n >= 3:
                    band_rows(n - 3)
                if n < len(items):
                    band_max(n)
                if n >= 14 and (n - 14) % 10 == 0:
                    band_mix_((n - 14) // 10)
            band_mix_(3)
            residual(CD_OUT, 1.0, 5)
            dve.wait_ge(conv_left, 16)
            ffn(3, 5)
            inv_rms(6)
            for m in range(DC):
                V.scalar_tensor_tensor(yout[:, m, :], x[:, m, :], par[:, P_FINAL + m:P_FINAL + m + 1], rstd[:],
                                       ALU.mult, ALU.mult).then_inc(y_ready, 1)


def kernel(x_prompt, x_sample, state_ret, cache_sb_k, cache_sb_v, cache_band_k, cache_band_v,
           state_ssm, state_conv, norm_g, ffn_w_in, ffn_w_out, final_g, w_in_ab, ret_gain, w_out_ab,
           w_in_cd, rel_bias, conv_w, conv_b, dt_bias, a_log, d_skip, ssd_gain, w_out_cd):
    import concourse.bacc as bacc
    from concourse.bass_utils import run_bass_kernel_spmd

    f = lambda v: np.asarray(v)
    const, tab, ret_cdec = tables()

    def cols(v):
        return f(v).reshape(-1, P).T

    def pairs_of(w, order, K):
        w = f(w).reshape(K, P, -1, P)[:, :, order]
        w = w.reshape(K, P, len(order) // 2, 2, P).transpose(2, 1, 3, 0, 4)
        return np.ascontiguousarray(w).reshape(len(order) // 2, P, 2 * K * P)

    par = np.zeros((P, NPAR), np.float32)
    par[:, P_NORM:P_NORM + 48] = f(norm_g).reshape(6 * DC, P).T
    par[:, P_FINAL:P_FINAL + 8] = cols(final_g)
    par[:, P_RET:P_RET + 4] = cols(ret_gain)
    par[:, P_SSD:P_SSD + 4] = cols(ssd_gain)
    par[:, P_CW:P_CW + 32] = f(conv_w).reshape(TAPS * DC, P).T
    par[:, P_CB:P_CB + 8] = cols(conv_b)
    par[0:8, P_DTB] = f(dt_bias)[0]
    par[0:8, P_ALOG] = f(a_log)[0]
    par[:, P_DSKIP:P_DSKIP + 8] = f(d_skip)[0][None]
    par[:, P_EPS] = EPS
    par[:, P_EPS + 1] = 1.0

    xcat = np.concatenate([f(x_prompt)[0], f(x_sample)[0]], 0)
    wi, wo = f(ffn_w_in).reshape(4, D, 2 * FF), f(ffn_w_out).reshape(4, FF, D)
    order = [[b for j in range(g * GC, (g + 1) * GC) for b in (j, FC + j)] for g in range(G)]
    wf_in = np.stack([np.stack([pairs_of(wi[i], order[g], DC) for g in range(G)]) for i in range(4)])
    wf_out = np.stack([np.stack([pairs_of(wo[i, g * GC * P:(g + 1) * GC * P], list(range(DC)), GC)
                                 for g in range(G)]) for i in range(4)])
    ab = [4, 5, 6, 7, 20, 21, 22, 23, 0, 1, 2, 3, 8, 9, 10, 11] + list(range(12, 20))
    cd = [8, 9, 10, 11] + list(range(16, 24)) + list(range(12, 16)) + list(range(0, 8))
    wcd = f(w_in_cd)[0]
    w_dt = np.zeros((D, P), np.float32)
    w_dt[:, 0:SSD_H] = wcd[:, 24 * P:]
    wcdo = f(w_out_cd)[0].reshape(2, 512, D)[::-1].reshape(D, D)

    def keys_t(v):
        return np.ascontiguousarray(f(v)[0, 0].reshape(PAST, 4, P).transpose(2, 1, 0))

    def vals(v):
        return np.ascontiguousarray(f(v)[0, 0].reshape(2, P, 512).transpose(1, 0, 2))

    ext = np.pad(f(rel_bias)[0][:, 1:257], ((0, 0), (0, 383)), mode="edge")
    idx = np.arange(P)[:, None] - np.arange(512)[None, :] + 511
    arrays = {
        "x": np.ascontiguousarray(xcat.T).reshape(DC, P, T),
        "const": const, "tab": tab, "par": par,
        "wf_in": wf_in, "wf_out": wf_out,
        "w_ab": pairs_of(f(w_in_ab)[0], ab, DC),
        "w_abo": pairs_of(f(w_out_ab)[0], list(range(DC)), DC),
        "w_cd": pairs_of(wcd[:, :24 * P], cd, DC),
        "w_dt": np.ascontiguousarray(w_dt.reshape(DC, P, P).transpose(1, 0, 2)).reshape(1, P, DC * P),
        "w_cdo": pairs_of(wcdo, list(range(DC)), DC),
        "kc": keys_t(cache_sb_k), "vc": vals(cache_sb_v), "kb": keys_t(cache_band_k), "vb": vals(cache_band_v),
        "s_ret": np.ascontiguousarray(f(state_ret)[0, 0].reshape(2, P, P).transpose(1, 0, 2)),
        "s_ssm": np.ascontiguousarray(f(state_ssm)[0, 0].transpose(2, 0, 1)).reshape(P, 512),
        "conv": np.ascontiguousarray(f(state_conv)[0, 0].reshape(3, DC, P).transpose(2, 1, 0)),
        "bias": np.ascontiguousarray(ext[:, idx].transpose(1, 0, 2)),
    }
    out_shapes = {
        "y": (DC, P, T), "sk": (4, P, T), "sv": (4, P, T), "bk": (4, P, T), "bv": (4, P, T),
        "p_ret": (P, 2, P), "s_ret": (P, 2, P), "ssm": (P, 2, 512), "conv": (P, DC, 2, 3),
    }
    nc = bacc.Bacc("TRN2", target_bir_lowering=False, num_devices=1)
    ins = {k: nc.dram_tensor("in_" + k, v.shape, F32, kind="ExternalInput").ap() for k, v in arrays.items()}
    outs = {k: nc.dram_tensor("out_" + k, v, F32, kind="ExternalOutput").ap() for k, v in out_shapes.items()}
    trunk(nc, ins, outs, ret_cdec)
    r = run_bass_kernel_spmd(nc, [{"in_" + k: v for k, v in arrays.items()}], core_ids=[0]).results[0]
    o = {k: np.asarray(r["out_" + k]) for k in out_shapes}

    y = o["y"].reshape(D, T).T
    rows = {k: o[k].reshape(512, T).T for k in ("sk", "sv", "bk", "bv")}

    def part(k, lo, hi):
        return np.ascontiguousarray(rows[k][lo:hi]).reshape(1, 1, hi - lo, 8, 64)

    def ret(v):
        return np.ascontiguousarray(v.transpose(1, 0, 2)).reshape(1, 1, RET_H, RET_DK, RET_DV)

    def ssm(v):
        return np.ascontiguousarray(v.reshape(SSD_N, SSD_H, SSD_P).transpose(1, 2, 0))[None, None]

    def conv(v):
        return np.ascontiguousarray(v.transpose(2, 1, 0)).reshape(1, 1, 3, D)

    return (np.ascontiguousarray(y[:LP])[None], np.ascontiguousarray(y[LP:])[None],
            ret(o["p_ret"]), part("sk", 0, LP), part("sv", 0, LP), part("bk", 0, LP), part("bv", 0, LP),
            ssm(o["ssm"][:, 0]), conv(o["conv"][:, :, 0]),
            ret(o["s_ret"]), part("sk", LP, T), part("sv", LP, T), part("bk", LP, T), part("bv", LP, T),
            ssm(o["ssm"][:, 1]), conv(o["conv"][:, :, 1]))
```
